# Optimizing a Trainium2 kernel written in Bass

```python
import math
import jax
import jax.numpy as jnp
from jax import lax
import numpy as np

D_MODEL = 1024
BATCH = 1
SEQ = 4096
DEPTH = 1

CHUNK = 64
N_META = 16
D_MIX = D_MODEL
CONV_WIDTH = 4
LRU_WIDTH = D_MIX // 2
LRU_BLOCKS = 8
LRU_BLOCK = LRU_WIDTH // LRU_BLOCKS
LRU_C = 8.0
DN_HEADS = 4
DN_HEAD_DIM = (D_MIX - LRU_WIDTH) // DN_HEADS
DN_WIDTH = DN_HEADS * DN_HEAD_DIM
N_GROUPS = 4
EXPERTS_PER_GROUP = 8
N_EXPERTS = N_GROUPS * EXPERTS_PER_GROUP
TOP_K = 2
D_EXPERT = D_MODEL // 4
MOE_BLOCK = 256
EPS = 1e-6
PROJ_WIDTH = 2 * LRU_WIDTH + 4 * DN_WIDTH + 2 * DN_HEADS

kernel_name = 'hymba_rglru_gdn_hier_moe_block'

def rmsnorm(x, g):
    xf = x.astype(jnp.float32)
    y = xf * lax.rsqrt(jnp.mean(xf * xf, axis=-1, keepdims=True) + EPS)
    return (y * g.astype(jnp.float32)).astype(x.dtype)

def l2norm(t):
    return t * lax.rsqrt(jnp.sum(t * t, axis=-1, keepdims=True) + EPS)

def causal_depthwise_conv(x, w):
    c = x.shape[-1]
    return lax.conv_general_dilated(
        x, w[:, None, :].astype(x.dtype), window_strides=(1,),
        padding=[(CONV_WIDTH - 1, 0)], dimension_numbers=('NWC', 'WIO', 'NWC'),
        feature_group_count=c)

def rglru_group(xb, gb, conv_w, conv_b, w_r, b_r, w_i, b_i, lam):
    bsz, t, _ = xb.shape
    xc = (causal_depthwise_conv(xb, conv_w) + conv_b.astype(xb.dtype)).astype(jnp.float32)
    xblk = xc.reshape(bsz, t, LRU_BLOCKS, LRU_BLOCK)
    r = jax.nn.sigmoid(jnp.einsum('btnc,ncd->btnd', xblk, w_r.astype(jnp.float32)).reshape(bsz, t, LRU_WIDTH) + b_r.astype(jnp.float32))
    i = jax.nn.sigmoid(jnp.einsum('btnc,ncd->btnd', xblk, w_i.astype(jnp.float32)).reshape(bsz, t, LRU_WIDTH) + b_i.astype(jnp.float32))
    log_a = -LRU_C * r * jax.nn.softplus(-lam.astype(jnp.float32))
    a = jnp.exp(log_a)
    b = jnp.sqrt(-jnp.expm1(2.0 * log_a)) * (i * xc)

    def combine(c1, c2):
        a1, b1 = c1
        a2, b2 = c2
        return a1 * a2, a2 * b1 + b2

    _, h = lax.associative_scan(combine, (a, b), axis=1)
    return (h * jax.nn.gelu(gb.astype(jnp.float32))).astype(xb.dtype)

def to_chunks(t, n_chunks):
    b, _, h = t.shape[:3]
    t = t.reshape((b, n_chunks, CHUNK, h) + t.shape[3:])
    return jnp.moveaxis(t, 3, 1)

def gated_deltanet_group(q, k, v, z, beta_logit, a_logit, conv_w, a_log, dt_bias, out_norm):
    bsz, t, _ = q.shape
    f32 = jnp.float32
    qkv = jax.nn.silu(causal_depthwise_conv(jnp.concatenate([q, k, v], axis=-1), conv_w)).astype(f32)
    q, k, v = jnp.split(qkv, 3, axis=-1)
    heads = lambda u: u.reshape(bsz, t, DN_HEADS, DN_HEAD_DIM)
    q = l2norm(heads(q)) * (DN_HEAD_DIM ** -0.5)
    k = l2norm(heads(k))
    v = heads(v)
    beta = jax.nn.sigmoid(beta_logit.astype(f32))
    g = -jnp.exp(a_log.astype(f32)) * jax.nn.softplus(a_logit.astype(f32) + dt_bias.astype(f32))

    pad = (-t) % CHUNK
    padf = lambda u: jnp.pad(u, [(0, 0), (pad, 0)] + [(0, 0)] * (u.ndim - 2))
    n_chunks = (t + pad) // CHUNK
    q, k, v = (to_chunks(padf(u), n_chunks) for u in (q, k, v))
    beta, g = (to_chunks(padf(u), n_chunks) for u in (beta, g))

    G = jnp.cumsum(g, axis=-1)
    causal = jnp.tril(jnp.ones((CHUNK, CHUNK), dtype=bool))
    strict = jnp.tril(jnp.ones((CHUNK, CHUNK), dtype=bool), k=-1)
    decay = jnp.exp(jnp.where(causal, G[..., :, None] - G[..., None, :], -jnp.inf))
    kk = jnp.einsum('bhncd,bhnsd->bhncs', k, k)
    A = jnp.where(strict, kk * decay * beta[..., :, None], 0.0)
    rhs = jnp.concatenate([v * beta[..., None], k * (beta * jnp.exp(G))[..., None]], axis=-1)
    sol = lax.linalg.triangular_solve(A, rhs, left_side=True, lower=True, unit_diagonal=True)
    u_c, w_c = sol[..., :DN_HEAD_DIM], sol[..., DN_HEAD_DIM:]
    qk = jnp.einsum('bhncd,bhnsd->bhncs', q, k) * decay
    q_dec = q * jnp.exp(G)[..., None]
    G_last = G[..., -1]
    k_dec = k * jnp.exp(G_last[..., None] - G)[..., None]

    def step(S, inp):
        qk_i, qd_i, kd_i, u_i, w_i, gl_i = inp
        v_new = u_i - jnp.einsum('bhcd,bhde->bhce', w_i, S)
        o = jnp.einsum('bhcd,bhde->bhce', qd_i, S) + jnp.einsum('bhcs,bhse->bhce', qk_i, v_new)
        S = S * jnp.exp(gl_i)[..., None, None] + jnp.einsum('bhcd,bhce->bhde', kd_i, v_new)
        return S, o

    xs = tuple(jnp.moveaxis(u, 2, 0) for u in (qk, q_dec, k_dec, u_c, w_c, G_last))
    S0 = jnp.zeros((bsz, DN_HEADS, DN_HEAD_DIM, DN_HEAD_DIM), f32)
    _, o = lax.scan(step, S0, xs)
    o = jnp.transpose(o, (1, 0, 3, 2, 4)).reshape(bsz, n_chunks * CHUNK, DN_HEADS, DN_HEAD_DIM)[:, pad:]
    o = rmsnorm(o, out_norm) * jax.nn.silu(heads(z.astype(f32)))
    return o.reshape(bsz, t, DN_WIDTH).astype(z.dtype)

def hybrid_mixer(u, w_in, lru_conv_w, lru_conv_b, lru_w_r, lru_b_r, lru_w_i, lru_b_i, lru_lambda,
                 lru_out_norm, dn_conv_w, dn_a_log, dn_dt_bias, dn_out_norm, w_out):
    proj = u @ w_in.astype(u.dtype)
    sizes = [LRU_WIDTH, LRU_WIDTH, DN_WIDTH, DN_WIDTH, DN_WIDTH, DN_WIDTH, DN_HEADS]
    xb, gb, q, k, v, z, b_logit, a_logit = jnp.split(proj, [int(s) for s in np.cumsum(sizes)], axis=-1)
    y_lru = rmsnorm(rglru_group(xb, gb, lru_conv_w, lru_conv_b, lru_w_r, lru_b_r, lru_w_i, lru_b_i, lru_lambda), lru_out_norm)
    y_dn = gated_deltanet_group(q, k, v, z, b_logit, a_logit, dn_conv_w, dn_a_log, dn_dt_bias, dn_out_norm)
    return jnp.concatenate([y_lru, y_dn], axis=-1) @ w_out.astype(u.dtype)

def hierarchical_moe(u, group_w, group_b, expert_w, expert_b, w_gate, w_up, w_down):
    bsz, t, d = u.shape
    n = bsz * t
    xf = u.reshape(n, d)
    p_group = jax.nn.softmax((xf @ group_w.astype(xf.dtype)).astype(jnp.float32) + group_b.astype(jnp.float32), axis=-1)
    p_sel, g_sel = lax.top_k(p_group, 1)
    e_logits = ((xf @ expert_w.astype(xf.dtype)).astype(jnp.float32) + expert_b.astype(jnp.float32)).reshape(n, N_GROUPS, EXPERTS_PER_GROUP)
    sel_logits = e_logits[jnp.arange(n), g_sel[:, 0]]
    top_logits, top_idx = lax.top_k(sel_logits, TOP_K)
    gates = (p_sel * jax.nn.softmax(top_logits, axis=-1)).reshape(-1)
    expert_ids = (g_sel * EXPERTS_PER_GROUP + top_idx).reshape(-1).astype(jnp.int32)
    token_ids = jnp.repeat(jnp.arange(n, dtype=jnp.int32), TOP_K)

    n_assign = n * TOP_K
    one_hot = (expert_ids[:, None] == jnp.arange(N_EXPERTS, dtype=jnp.int32)[None, :]).astype(jnp.int32)
    counts = jnp.sum(one_hot, axis=0)
    rank = jnp.cumsum(one_hot, axis=0)[jnp.arange(n_assign), expert_ids] - 1
    padded = (counts + MOE_BLOCK - 1) // MOE_BLOCK * MOE_BLOCK
    ends = jnp.cumsum(padded)
    dest = (ends - padded)[expert_ids] + rank
    n_blocks = -(-(n_assign + N_EXPERTS * (MOE_BLOCK - 1)) // MOE_BLOCK)
    cap = n_blocks * MOE_BLOCK
    buf_tok = jnp.full((cap,), n, jnp.int32).at[dest].set(token_ids)
    buf_gate = jnp.zeros((cap,), jnp.float32).at[dest].set(gates)
    block_start = jnp.arange(n_blocks, dtype=jnp.int32) * MOE_BLOCK
    block_expert = jnp.minimum(jnp.sum(block_start[:, None] >= ends[None, :], axis=1), N_EXPERTS - 1)
    x_pad = jnp.concatenate([xf, jnp.zeros((1, d), xf.dtype)], axis=0)
    x_buf = x_pad[buf_tok].reshape(n_blocks, MOE_BLOCK, d)

    def expert_block(args):
        xb, e = args
        h = jax.nn.silu(xb @ w_gate[e].astype(xb.dtype)) * (xb @ w_up[e].astype(xb.dtype))
        return h @ w_down[e].astype(xb.dtype)

    y = lax.map(expert_block, (x_buf, block_expert)).reshape(cap, d)
    y = y * buf_gate[:, None].astype(y.dtype)
    out = jnp.zeros((n + 1, d), y.dtype).at[buf_tok].add(y)[:n]
    return out.reshape(bsz, t, d)

def setup_inputs(seed: int = 0) -> dict:
    key = jax.random.key(seed)
    ks = iter(jax.random.split(key, 40))
    f32 = jnp.float32
    nrm = lambda shape, scale: scale * jax.random.normal(next(ks), shape, f32)
    L = DEPTH
    x = nrm((BATCH, SEQ, D_MODEL), 1.0)
    meta_tokens = nrm((N_META, D_MODEL), 1.0)
    mix_norm = 1.0 + nrm((L, D_MODEL), 0.02)
    w_in = nrm((L, D_MODEL, PROJ_WIDTH), D_MODEL ** -0.5)
    lru_conv_w = nrm((L, CONV_WIDTH, LRU_WIDTH), CONV_WIDTH ** -0.5)
    lru_conv_b = nrm((L, LRU_WIDTH), 0.02)
    lru_w_r = nrm((L, LRU_BLOCKS, LRU_BLOCK, LRU_BLOCK), LRU_BLOCK ** -0.5)
    lru_b_r = nrm((L, LRU_WIDTH), 0.02)
    lru_w_i = nrm((L, LRU_BLOCKS, LRU_BLOCK, LRU_BLOCK), LRU_BLOCK ** -0.5)
    lru_b_i = nrm((L, LRU_WIDTH), 0.02)
    a_pow = jax.random.uniform(next(ks), (L, LRU_WIDTH), f32, 0.9, 0.999)
    a_base = a_pow ** (1.0 / LRU_C)
    lru_lambda = jnp.log(a_base) - jnp.log1p(-a_base)
    lru_out_norm = 1.0 + nrm((L, LRU_WIDTH), 0.02)
    dn_conv_w = nrm((L, CONV_WIDTH, 3 * DN_WIDTH), CONV_WIDTH ** -0.5)
    dn_a_log = jnp.log(jax.random.uniform(next(ks), (L, DN_HEADS), f32, 1.0, 16.0))
    dt = jnp.exp(jax.random.uniform(next(ks), (L, DN_HEADS), f32, math.log(1e-3), math.log(1e-1)))
    dn_dt_bias = dt + jnp.log(-jnp.expm1(-dt))
    dn_out_norm = 1.0 + nrm((L, DN_HEAD_DIM), 0.02)
    w_out = nrm((L, D_MIX, D_MODEL), D_MIX ** -0.5)
    ffn_norm = 1.0 + nrm((L, D_MODEL), 0.02)
    router_group_w = nrm((L, D_MODEL, N_GROUPS), D_MODEL ** -0.5)
    router_group_b = nrm((L, N_GROUPS), 0.01)
    router_expert_w = nrm((L, D_MODEL, N_EXPERTS), D_MODEL ** -0.5)
    router_expert_b = nrm((L, N_EXPERTS), 0.01)
    moe_w_gate = nrm((L, N_EXPERTS, D_MODEL, D_EXPERT), D_MODEL ** -0.5)
    moe_w_up = nrm((L, N_EXPERTS, D_MODEL, D_EXPERT), D_MODEL ** -0.5)
    moe_w_down = nrm((L, N_EXPERTS, D_EXPERT, D_MODEL), D_EXPERT ** -0.5)
    final_norm = 1.0 + nrm((D_MODEL,), 0.02)
    return {'x': x, 'meta_tokens': meta_tokens, 'mix_norm': mix_norm, 'w_in': w_in,
            'lru_conv_w': lru_conv_w, 'lru_conv_b': lru_conv_b, 'lru_w_r': lru_w_r, 'lru_b_r': lru_b_r,
            'lru_w_i': lru_w_i, 'lru_b_i': lru_b_i, 'lru_lambda': lru_lambda, 'lru_out_norm': lru_out_norm,
            'dn_conv_w': dn_conv_w, 'dn_a_log': dn_a_log, 'dn_dt_bias': dn_dt_bias, 'dn_out_norm': dn_out_norm,
            'w_out': w_out, 'ffn_norm': ffn_norm, 'router_group_w': router_group_w, 'router_group_b': router_group_b,
            'router_expert_w': router_expert_w, 'router_expert_b': router_expert_b,
            'moe_w_gate': moe_w_gate, 'moe_w_up': moe_w_up, 'moe_w_down': moe_w_down, 'final_norm': final_norm}

def reference(x, meta_tokens, mix_norm, w_in, lru_conv_w, lru_conv_b, lru_w_r, lru_b_r, lru_w_i, lru_b_i,
              lru_lambda, lru_out_norm, dn_conv_w, dn_a_log, dn_dt_bias, dn_out_norm, w_out, ffn_norm,
              router_group_w, router_group_b, router_expert_w, router_expert_b, moe_w_gate, moe_w_up,
              moe_w_down, final_norm):
    bsz = x.shape[0]
    meta = jnp.broadcast_to(meta_tokens.astype(x.dtype)[None], (bsz, N_META, D_MODEL))
    h = jnp.concatenate([meta, x], axis=1)
    for l in range(DEPTH):
        h = h + hybrid_mixer(rmsnorm(h, mix_norm[l]), w_in[l], lru_conv_w[l], lru_conv_b[l], lru_w_r[l],
                             lru_b_r[l], lru_w_i[l], lru_b_i[l], lru_lambda[l], lru_out_norm[l],
                             dn_conv_w[l], dn_a_log[l], dn_dt_bias[l], dn_out_norm[l], w_out[l])
        h = h + hierarchical_moe(rmsnorm(h, ffn_norm[l]), router_group_w[l], router_group_b[l],
                                 router_expert_w[l], router_expert_b[l], moe_w_gate[l], moe_w_up[l], moe_w_down[l])
    h = rmsnorm(h, final_norm)
    return h[:, N_META:]


_drawn_inputs = setup_inputs


def setup_inputs(seed=0):
    import zlib

    import numpy as np

    out = dict(_drawn_inputs(seed))
    spreads = {}
    factors = {'lru_b_r': 7.131,
     'lru_b_i': 5.598,
     'lru_out_norm': 9.138,
     'dn_out_norm': 15.857,
     'router_group_b': 25.165,
     'router_expert_b': 26.866,
     'final_norm': 7.83,
     'ffn_norm': 5.122}
    for name, (base, spread) in spreads.items():
        noise = np.random.default_rng([zlib.crc32(name.encode()), seed]).standard_normal(out[name].shape)
        drawn = base * np.exp(spread * noise) if base else spread * noise
        out[name] = jnp.asarray(drawn.astype(out[name].dtype))
    for name, factor in factors.items():
        out[name] = (out[name] * factor).astype(out[name].dtype)
    return out
```

```python
from contextlib import ExitStack

import concourse.bass as bass
from concourse import mybir

P = 128
D = 1024
SEQ = 4096
META = 16
PAD = P - META
TILES = SEQ // P + 1
KT = D // P
LRU = 512
H = 4
CW = 4
PROJ = 3080
NG = 4
EPG = 8
NE = NG * EPG
FE = 256
EPS = 1e-6
LEVELS = range(2, 8)
NBLK = (2 * SEQ + NE * (P - 1)) // P
TCAP = SEQ
WSLOTS = 4
GU = 2 * KT * FE
WD = 2 * D
SLOT = GU + WD
RSTEPS = 20

ALU = mybir.AluOpType
ACT = mybir.ActivationFunctionType
AX = mybir.AxisListType.X
F32 = mybir.dt.float32
BF16 = mybir.dt.bfloat16
I32 = mybir.dt.int32
U32 = mybir.dt.uint32

COL = {"xb": 0, "gb": 512, "q": 1024, "k": 1536, "v": 2048, "z": 2560, "ba": 3072}
GROUPS = ["xb", "q", "k", "v", "gb", "z"]
LOOP = (4, TILES - 2)


def bcast(ap, shape):
    return ap.to_broadcast(shape)


class Step:

    def __init__(self, i):
        self.i = i
        self.F, self.nF, self.pF = self.counts(i + 3, TILES)
        self.P, self.nP, self.pP = self.counts(i + 2, TILES)
        self.G, self.nG, self.pG = self.counts(i + 1, TILES)
        self.O, self.nO, self.pO = self.counts(i - 1, TILES - 1)
        self.R, self.nR, self.pR = self.counts(i - 2, TILES - 1)

    @staticmethod
    def counts(n, most):
        if not isinstance(n, int):
            return True, n, n - 1
        after, before = min(max(n, 0), most), min(max(n - 1, 0), most)
        return after != before, after, before


def steps(eng, body):
    for i in range(-2, LOOP[0]):
        body(Step(i))
    with eng.Fori(LOOP[0], LOOP[1]) as i:
        body(Step(i))
    for i in range(LOOP[1], TILES + 2):
        body(Step(i))


def need(eng, sem, value):
    if not (isinstance(value, int) and value <= 0):
        eng.wait_ge(sem, value)


def hymba_block(nc, xm, w_in, w_out, conv_w, lru_cols, w_r, w_i, mix_g, ffn_g, final_g, dn_g, dn_a,
                dn_dt, w_router, b_router, w_gate, w_up, w_down, out):
    with ExitStack() as ctx:
        def sb(name, shape, dt=F32):
            return ctx.enter_context(nc.sbuf_tensor(name, shape, dt))

        sems = {}

        def sem(name):
            if name not in sems:
                sems[name] = nc.alloc_semaphore(name=name)
            return sems[name]

        def settle(eng):
            eng.sem_inc(sem("settled"), 1)

        def retire(keep):
            nc.all_engine_barrier()
            done = {n: s for n, s in sems.items() if n not in keep}
            nums = sorted(s.num for s in done.values())
            runs = [[nums[0], nums[0] + 1]]
            for n in nums[1:]:
                if n == runs[-1][1]:
                    runs[-1][1] += 1
                else:
                    runs.append([n, n + 1])
            for a, b in runs:
                nc.sync.sem_clear(range(a, b))
            nc.all_engine_barrier()
            for n, s in done.items():
                nc.release_semaphore(s)
                del sems[n]

        h_rows = nc.dram_tensor("h_rows", [SEQ, D], F32, kind="Internal").ap()
        y_rows = nc.dram_tensor("y_rows", [NBLK * P, D], F32, kind="Internal").ap()
        idx_tab = nc.dram_tensor("idx_tab", [NE * TCAP, 1], I32, kind="Internal").ap()
        blk_tab = nc.dram_tensor("blk_tab", [P, 3], I32, kind="Internal").ap()

        W = sb("W", [P, KT * PROJ + KT * D])
        wi = W[:, 0:KT * PROJ].rearrange("p (k n) -> p k n", k=KT)
        wo = W[:, KT * PROJ:KT * PROJ + KT * D].rearrange("p (k n) -> p k n", k=KT)
        wr_bd = sb("wr_bd", [P, 4, P])
        wi_bd = sb("wi_bd", [P, 4, P])
        w_rt = sb("w_rt", [P, KT, NG + NE])

        ident = sb("ident", [P, P])
        ones = sb("ones", [P, P])
        tri = sb("tri", [P, P])
        tri_s = sb("tri_s", [P, P])
        lvl = sb("lvl", [P, 7, P])
        cvw = sb("cvw", [P, 16, CW])
        lcol = sb("lcol", [P, 5, 4])
        cl = sb("cl", [P, 4])
        cl_t = sb("cl_t", [P, 4])
        mg = sb("mg", [P, KT])
        fg = sb("fg", [P, KT])
        dng = sb("dng", [P, P])
        nexp_a = sb("nexp_a", [P, H])
        dt_b = sb("dt_b", [P, H])
        rb = sb("rb", [P, NG + NE])
        eps = sb("eps", [P, 1])
        tiny = sb("tiny", [P, 1])
        iota_e = sb("iota_e", [P, NE])
        iota_p = sb("iota_p", [P, 1])
        io_i = sb("io_i", [P, NE], I32)
        ip_i = sb("ip_i", [P, 1], I32)

        x_in = sb("x_in", [P, D])
        uT = sb("uT", [P, KT, P])
        junk = sb("junk", [P, D], BF16)
        xst = sb("xst", [P, 3])
        ext = [sb(f"ext_{g}", [P, 4, P + 3]) for g in ("xb", "q", "k", "v")]
        xc, qs, ks, vs = (sb(n, [P, 4, P]) for n in ("xc", "qs", "ks", "vs"))
        hT = sb("hT", [P, KT, P])
        la, th = hT[:, 0:4, :], hT[:, 4:8, :]
        gx = sb("gx", [P, 4, P])
        gg = sb("gg", [P, 4, P])
        zg = sb("zg", [P, 4, P])
        sgb = sb("sgb", [P, H])
        al = sb("al", [P, H])
        rnq = sb("rnq", [P, 4, P])
        rnk = sb("rnk", [P, 4, P])
        qh = sb("qh", [P, 4, P])
        kh = sb("kh", [P, 4, P])
        vn, ot, Y = rnq, rnk, qh
        dec = sb("dec", [P, 4, P])
        T = dec
        Mt = sb("Mt", [P, 4, P])
        ML = [sb(f"ML{n}", [P, 4, P]) for n in range(2)]
        X = sb("X", [P, 4, P])
        kd = sb("kd", [P, 4, P])
        vt = sb("vt", [P, 4, P])
        qkT = sb("qkT", [P, 4, P])
        yt = sb("yt", [P, 4, P])
        St = sb("St", [P, 4, P])
        beta = sb("beta", [P, H])
        g4 = sb("g4", [P, H])
        ga = sb("ga", [P, H])
        gl8 = sb("gl8", [P, 8])
        eg8 = sb("eg8", [P, 8])
        neg = sb("neg", [P, H])
        ekd = sb("ekd", [P, H])
        oss = sb("oss", [P, H])
        ors = sb("ors", [P, H])
        aa = sb("aa", [P, 4, P])
        hh = sb("hh", [P, 4, P])
        hlast = sb("hlast", [P, 4])
        lrs = sb("lrs", [P, P])
        yl = sb("yl", [P, 4, P])
        ydT = yt
        ht = sb("ht", [P, D])
        hst = sb("hst", [P, 3])
        lg = sb("lg", [P, NG + NE])
        rg8 = sb("rg8", [P, 8])
        m8 = sb("m8", [P, 8])
        i8 = sb("i8", [P, 8], U32)
        v8 = sb("v8", [P, 8])
        j8 = sb("j8", [P, 8], U32)
        rsm = sb("rsm", [P, 16])
        eg = sb("eg", [P, NG])
        ohg = sb("ohg", [P, NG])
        elg = sb("elg", [P, EPG, NG])
        el8 = sb("el8", [P, EPG])
        oh = sb("oh", [P, 2, NE])
        ohs = sb("ohs", [P, NE])
        pre = sb("pre", [P, NE])
        jr = sb("jr", [P, NE])
        cnt = sb("cnt", [P, NE])
        rt6 = sb("rt6", [P, 6])
        posf = sb("posf", [P, 2])
        posi = sb("posi", [P, 2], I32)
        tokf = sb("tokf", [P, 1])
        toki = sb("toki", [P, 1], I32)
        saved = sb("saved", [P, SEQ // P, 6])

        pj = [ctx.enter_context(nc.psum_tensor(f"pj{n}", [P, 4, P], F32)) for n in range(2)]
        bA = ctx.enter_context(nc.psum_tensor("bA", [P, 4, P], F32))
        bB = ctx.enter_context(nc.psum_tensor("bB", [P, 4, P], F32))
        bC = ctx.enter_context(nc.psum_tensor("bC", [P, 4, P], F32))
        bT = ctx.enter_context(nc.psum_tensor("bT", [P, 4, P], F32))
        bO = ctx.enter_context(nc.psum_tensor("bO", [P, 8, P], F32))
        bTf = bT[:].rearrange("p a b -> p (a b)")
        bOf = bO[:].rearrange("p a b -> p (a b)")

        with nc.Block() as block:
            @block.sync
            def _(sp):
                sp.dma_start(wi, w_in.rearrange("(p k) n -> p k n", k=KT)).then_inc(sem("w_in_in"), 16)
                sp.dma_start(wo, w_out.rearrange("(k p) n -> p k n", p=P)).then_inc(sem("w_out_in"), 16)
                sp.dma_start(w_rt[:], w_router.rearrange("(p k) n -> p k n", k=KT)).then_inc(sem("w_rt_in"), 16)
                sp.wait_ge(sem("w_in_in"), 16)
                sp.wait_ge(sem("w_out_in"), 16)
                sp.wait_ge(sem("w_rt_in"), 16)

            @block.scalar
            def _(act):
                n = 0
                for dst, src in ((cvw[:], conv_w), (lcol[:], lru_cols), (mg[:], mix_g), (fg[:], ffn_g),
                                 (dng[:], dn_g.partition_broadcast(P)), (nexp_a[:], dn_a.partition_broadcast(P)),
                                 (dt_b[:], dn_dt.partition_broadcast(P)), (rb[:], b_router.partition_broadcast(P))):
                    act.dma_start(dst, src).then_inc(sem("small_in"), 16)
                    n += 16
                act.wait_ge(sem("blocks_zero"), 1)
                for dst, src in ((wr_bd, w_r), (wi_bd, w_i)):
                    pair = src.rearrange("(j b) c d -> b c j d", b=2)
                    for b in range(2):
                        act.dma_start(dst[64 * b:64 * b + 64, :, 64 * b:64 * b + 64], pair[b]).then_inc(sem("bd_in"), 16)
                act.wait_ge(sem("small_in"), n)
                act.wait_ge(sem("bd_in"), 64)
                nc.scalar.activation(nexp_a[:], nexp_a[:], ACT.Exp).then_inc(sem("exp_a"), 1)
                nc.scalar.activation(cl[:], lcol[:, 3, :], ACT.Abs).then_inc(sem("cl_s"), 1)
                act.wait_ge(sem("cl_s"), 1)
                nc.scalar.activation(cl[:], cl[:], ACT.Exp, scale=-1.0).then_inc(sem("cl_s"), 1)
                act.wait_ge(sem("cl_s"), 2)
                nc.scalar.activation(cl[:], cl[:], ACT.Ln, bias=1.0).then_inc(sem("cl_s"), 1)

            @block.vector
            def _(dve):
                for t in ext:
                    nc.vector.memset(t[:], 0.0)
                nc.vector.memset(St[:], 0.0)
                nc.vector.memset(hlast[:], 0.0)
                nc.vector.memset(cnt[:], 0.0)
                nc.vector.memset(rg8[:], -3.0e38)
                nc.vector.memset(eps[:], EPS)
                nc.vector.memset(tiny[:], 1e-19).then_inc(sem("dve_const"), 1)
                dve.wait_ge(sem("exp_a"), 1)
                nc.vector.tensor_scalar(nexp_a[:], nexp_a[:], -1.0, None, ALU.mult).then_inc(sem("nexp"), 1)
                dve.wait_ge(sem("cl_s"), 3)
                nc.vector.tensor_scalar(cl_t[:], lcol[:, 3, :], -1.0, 0.0, ALU.mult, ALU.max).then_inc(sem("cl_d"), 1)
                dve.wait_ge(sem("cl_d"), 1)
                nc.vector.tensor_tensor(cl[:], cl[:], cl_t[:], ALU.add).then_inc(sem("cl_d"), 1)
                dve.wait_ge(sem("cl_d"), 2)
                nc.vector.tensor_scalar(cl[:], cl[:], -8.0, None, ALU.mult).then_inc(sem("cl_d"), 1)
                dve.wait_ge(sem("iota_i"), 2)
                nc.vector.tensor_copy(iota_e[:], io_i[:])
                nc.vector.tensor_copy(iota_p[:], ip_i[:])
                nc.vector.tensor_copy(tokf[:], ip_i[:]).then_inc(sem("iota_f"), 1)
                dve.wait_ge(sem("iota_f"), 1)

            @block.gpsimd
            def _(pool):
                nc.gpsimd.memset(wr_bd[:], 0.0)
                nc.gpsimd.memset(wi_bd[:], 0.0).then_inc(sem("blocks_zero"), 1)
                nc.gpsimd.iota(io_i[:], pattern=[[1, NE]], base=0, channel_multiplier=0).then_inc(sem("iota_i"), 1)
                nc.gpsimd.iota(ip_i[:], pattern=[[0, 1]], base=0, channel_multiplier=1).then_inc(sem("iota_i"), 1)
                nc.gpsimd.memset(xc[:].bitcast(I32), 0).then_inc(sem("zero_i"), 1)
                nc.gpsimd.memset(ones[:], 1.0).then_inc(sem("p_const"), 1)
                pool.wait_ge(sem("zero_i"), 1)
                zt = xc[:].rearrange("p a b -> p (a b)").bitcast(I32)
                per = NE * TCAP // P
                for n in range(per // 512):
                    pool.dma_start(idx_tab.rearrange("(p n) o -> p (n o)", p=P)[:, 512 * n:512 * n + 512],
                                   zt).then_inc(sem("idx_zeroed"), 16)
                pool.wait_ge(sem("p_const"), 1)
                nc.gpsimd.affine_select(out=ident[:], in_=ones[:], compare_op=ALU.is_equal, fill=0.0, base=0,
                                        pattern=[[1, P]], channel_multiplier=-1).then_inc(sem("p_const"), 1)
                nc.gpsimd.affine_select(out=tri[:], in_=ones[:], compare_op=ALU.is_ge, fill=0.0, base=0,
                                        pattern=[[1, P]], channel_multiplier=-1).then_inc(sem("p_const"), 1)
                nc.gpsimd.affine_select(out=tri_s[:], in_=ones[:], compare_op=ALU.is_gt, fill=0.0, base=0,
                                        pattern=[[1, P]], channel_multiplier=-1).then_inc(sem("p_const"), 1)
                pool.wait_ge(sem("p_const"), 4)
                done = 4
                for l in range(1, 8):
                    b = 1 << l
                    m = lvl[:, l - 1, :]
                    mv = m.rearrange("p (n c) -> p n c", c=b)
                    src = tri_s[:].rearrange("p (n c) -> p n c", c=b)
                    nc.gpsimd.affine_select(out=mv, in_=src, compare_op=ALU.is_ge, fill=0.0, base=0,
                                            pattern=[[-b, P // b], [0, b]], channel_multiplier=1).then_inc(sem("p_const"), 1)
                    done += 1
                    pool.wait_ge(sem("p_const"), done)
                    nc.gpsimd.affine_select(out=mv, in_=mv, compare_op=ALU.is_ge, fill=0.0, base=b // 2 - 1,
                                            pattern=[[b, P // b], [0, b]], channel_multiplier=-1).then_inc(sem("p_const"), 1)
                    done += 1
                    pool.wait_ge(sem("p_const"), done)
                    nc.gpsimd.affine_select(out=mv, in_=mv, compare_op=ALU.is_ge, fill=0.0, base=-(b // 2),
                                            pattern=[[0, P // b], [1, b]], channel_multiplier=0).then_inc(sem("p_const"), 1)
                    done += 1
                    pool.wait_ge(sem("p_const"), done)
                pool.wait_ge(sem("idx_zeroed"), 16 * (per // 512))

        def flat(t):
            return t[:].rearrange("p a b -> p (a b)")

        def rows(t):
            return t.unsqueeze(2).to_broadcast([P, 4, P])

        def cols(t):
            return t.unsqueeze(1).to_broadcast([P, 4, P])

        with nc.Block() as block:
            @block.sync
            def _(sp):
                def body(s):
                    if s.F:
                        need(sp, sem("x_turned"), s.pF)
                        settle(sp)
                        sp.dma_start(x_in[:], xm[bass.ds((s.i + 2) * P, P), :]).then_inc(sem("x_in"), 16)
                    if s.O:
                        need(sp, sem("h_turned"), s.nR)
                        need(sp, sem("h_norm"), s.pO)
                        settle(sp)
                        need(sp, sem("h_stored"), 16 * s.pO)
                        settle(sp)
                        sp.dma_start(ht[:], xm[bass.ds(s.nO * P, P), :]).then_inc(sem("x_res"), 16)
                        need(sp, sem("h_ready"), s.nO)
                        settle(sp)
                        sp.dma_start(h_rows[bass.ds(s.pO * P, P), :], ht[:]).then_inc(sem("h_stored"), 16)
                steps(sp, body)
                sp.wait_ge(sem("h_stored"), 16 * (TILES - 1))

            @block.tensor
            def _(pe):
                def project(s, n):
                    if not s.P:
                        return
                    g, j = divmod(n, 4)
                    if n == 0:
                        need(pe, sem("uT_ready"), s.nP)
                    if j == 0:
                        free, v = (("gb_used", s.pP), ("z_used", s.pP), ("xb_evac", s.nP), ("q_evac", s.nP),
                                   ("k_evac", s.nP))[g]
                        need(pe, sem(free), v)
                    c = COL[GROUPS[g]] + j * P
                    for k in range(KT):
                        mm = pe.matmul(pj[g % 2][:, j, :], wi[:, k, c:c + P], uT[:, k, :], start=(k == 0), stop=(k == KT - 1))
                    if j == 3:
                        mm.then_inc(sem(GROUPS[g] + "_full"), 1)

                def project_z(s, n):
                    if not s.P:
                        return
                    if n == 0:
                        need(pe, sem("v_evac"), s.nP)
                    c = COL["z"]
                    for k in (2 * n, 2 * n + 1):
                        mm = pe.matmul(flat(pj[1]), uT[:, k, :], wi[:, k, c:c + 512], start=(k == 0), stop=(k == KT - 1))
                    if n == 3:
                        mm.then_inc(sem("z_full"), 1)

                def w_out_part(s, n):
                    if not s.O:
                        return
                    half, m = divmod(n, 4)
                    if n == 0:
                        need(pe, sem("ydT_ready"), s.nO)
                        need(pe, sem("yl_ready"), s.nO + 1)
                        need(pe, sem("hT_ready"), s.nR)
                        need(pe, sem("uT_ready"), s.pF)
                    for j in (2 * m, 2 * m + 1):
                        lhs = yl[:, j, :] if j < 4 else ydT[:, j - 4, :]
                        mm = pe.matmul(bOf[:, 512 * half:512 * half + 512], lhs, wo[:, j, 512 * half:512 * half + 512],
                                       start=(j == 0), stop=(j == 7))
                    if n == 7:
                        mm.then_inc(sem("wo_full"), 1)

                def fill(s, n):
                    if n < 8:
                        project(s, 12 + n)
                    elif n < 12:
                        project_z(s, n - 8)
                    else:
                        w_out_part(s, n - 12)

                def body(s):
                    if s.R:
                        need(pe, sem("h_ready"), s.nR)
                        need(pe, sem("uT_ready"), s.pF)
                        for k in range(KT):
                            mm = pe.transpose(bO[:, k, :], ht[:, k:D:KT], ident[:])
                        mm.then_inc(sem("h_turned"), 1)
                    if s.G:
                        need(pe, sem("sq_k"), s.nG)
                        need(pe, sem("r_gate"), s.pP)
                        pe.matmul(flat(bB), ones[:], flat(rnk), start=True, stop=True).then_inc(sem("nk_full"), 1)
                        need(pe, sem("sq_q"), s.nG)
                        need(pe, sem("S_new"), s.pG)
                        pe.matmul(flat(bA), ones[:], flat(rnq), start=True, stop=True).then_inc(sem("nq_full"), 1)
                    project(s, 0)
                    project(s, 1)
                    if s.G:
                        need(pe, sem("g_ready"), s.nG)
                        need(pe, sem("al_ready"), s.pP)
                        need(pe, sem("sgb_ready"), s.pP)
                        pe.matmul(bTf[:, 0:H], tri[:], g4[:], start=True, stop=True)
                        pe.matmul(bTf[:, H:2 * H], ones[:], g4[:], start=True, stop=True).then_inc(sem("cum_full"), 1)
                        need(pe, sem("gtri_ready"), s.nG)
                        need(pe, sem("i_gate"), s.pP)
                        pe.matmul(flat(bC), ones[:], flat(dec), start=True, stop=True).then_inc(sem("grow_full"), 1)
                    for n in (2, 3, 4, 5):
                        project(s, n)
                    if s.G:
                        need(pe, sem("kh_ready"), s.nG)
                        need(pe, sem("gl8_ready"), s.nG)
                        for h in range(H):
                            mm = pe.transpose(bT[:, h, :], kh[:, h, :], ident[:])
                        mm.then_inc(sem("kt_full"), 1)
                        need(pe, sem("qh_ready"), s.nG)
                        need(pe, sem("nq_used"), s.nG)
                        for h in range(H):
                            mm = pe.matmul(bA[:, h, :], kh[:, h, :], kh[:, h, :], start=True, stop=True)
                        mm.then_inc(sem("kk_full"), 1)
                        need(pe, sem("nk_used"), s.nG)
                        for h in range(H):
                            mm = pe.matmul(bB[:, h, :], kh[:, h, :], qh[:, h, :], start=True, stop=True)
                        mm.then_inc(sem("qk_full"), 1)
                        need(pe, sem("dec_sub"), s.nG)
                        need(pe, sem("v_silu"), s.nG)
                        for h in range(H):
                            mm = pe.transpose(bC[:, h, :], vs[:, h, :], ident[:])
                        mm.then_inc(sem("vt_full"), 1)
                    for n in (6, 7, 8):
                        project(s, n)
                    if s.O:
                        need(pe, sem("yt_ready"), s.nO + 1)
                        need(pe, sem("kd_ready"), s.nG)
                        if not s.G:
                            need(pe, sem("lrs_ln"), s.nG)
                        for h in range(H):
                            mm = pe.transpose(bT[:, h, :], yt[:, h, :], ident[:])
                        mm.then_inc(sem("ydT_full"), 1)
                    for n in (9, 10):
                        project(s, n)
                    if s.G:
                        need(pe, sem("X_first"), s.nG)
                        need(pe, sem("ydT_ready"), s.nO)
                        if not s.O:
                            need(pe, sem("kd_ready"), s.nG)
                        for h in range(H):
                            mm = pe.transpose(bT[:, h, :], X[:, h, :], ident[:])
                        mm.then_inc(sem("T_full"), 1)
                        need(pe, sem("vt_ready"), s.nG)
                        need(pe, sem("S_new"), s.pG)
                        for h in range(H):
                            mm = pe.matmul(bC[:, h, :], kh[:, h, :], St[:, h, :], start=True, stop=True)
                        mm.then_inc(sem("kS_full"), 1)
                        need(pe, sem("M_raw"), s.nG)
                        for h in range(H):
                            mm = pe.matmul(bA[:, h, :], qh[:, h, :], St[:, h, :], start=True, stop=True)
                        mm.then_inc(sem("qS_full"), 1)
                    project(s, 11)
                    if s.R:
                        need(pe, sem("hT_ready"), s.nR)
                        if s.G:
                            need(pe, sem("T_new"), 6 * s.pG + 1)
                        else:
                            need(pe, sem("ydT_ready"), s.nO)
                            need(pe, sem("rank_used"), s.pR)
                        for k in range(KT):
                            mm = pe.matmul(bTf[:, 0:NG + NE], hT[:, k, :], w_rt[:, k, :], start=(k == 0), stop=(k == KT - 1))
                        mm.then_inc(sem("rt_full"), 1)
                    for l in LEVELS:
                        n = 3 * (l - 2)
                        if s.G:
                            c = 6 * s.pG + l - 1
                            need(pe, sem("ML_ready"), c)
                            need(pe, sem("T_new"), c)
                            if l == 2:
                                need(pe, sem("o1_ready"), s.nG)
                            for h in range(H):
                                mm = pe.matmul(bA[:, h, :], ML[l % 2][:, h, :], T[:, h, :], start=True, stop=True)
                            mm.then_inc(sem("Y_full"), 1)
                        fill(s, n)
                        if s.G:
                            need(pe, sem("Y_new"), c)
                            need(pe, sem("qkT_ready"), s.nG) if l == 2 else need(pe, sem("X_new"), c - 1)
                            for h in range(H):
                                mm = pe.matmul(bB[:, h, :], Y[:, h, :], X[:, h, :], start=True, stop=True)
                            mm.then_inc(sem("XU_full"), 1)
                        fill(s, n + 1)
                        if l < 7:
                            if s.G:
                                need(pe, sem("X_new"), c)
                                if l == 2:
                                    need(pe, sem("lg_ready"), s.nR)
                                if l == 6:
                                    need(pe, sem("rank_used"), s.nR)
                                for h in range(H):
                                    mm = pe.transpose(bT[:, h, :], X[:, h, :], ident[:])
                                mm.then_inc(sem("T_full"), 1)
                            fill(s, n + 2)
                        if l == 5 and s.R:
                            need(pe, sem("oh_ready"), s.nR)
                            need(pe, sem("lg_ready"), s.nR)
                            if s.G:
                                need(pe, sem("T_new"), 6 * s.pG + 5)
                            pe.matmul(bTf[:, 0:NE], tri_s[:], ohs[:], start=True, stop=True)
                            pe.matmul(bTf[:, NE:2 * NE], ones[:], ohs[:], start=True, stop=True).then_inc(sem("rank_full"), 1)
                    if s.G:
                        need(pe, sem("R_ready"), s.nG)
                        need(pe, sem("X_new"), 6 * s.nG)
                        for h in range(H):
                            mm = pe.matmul(bB[:, h, :], X[:, h, :], vt[:, h, :], start=True, stop=True)
                        mm.then_inc(sem("vn_full"), 1)
                    fill(s, 17)
                    if s.G:
                        need(pe, sem("vn_ready"), s.nG)
                        for h in range(H):
                            mm = pe.matmul(bC[:, h, :], qkT[:, h, :], vn[:, h, :], start=True, stop=True)
                        mm.then_inc(sem("intra_full"), 1)
                        need(pe, sem("kd_ready"), s.nG)
                        need(pe, sem("Y_new"), 6 * s.nG)
                        for h in range(H):
                            mm = pe.matmul(bA[:, h, :], kd[:, h, :], vn[:, h, :], start=True, stop=True)
                        mm.then_inc(sem("Su_full"), 1)
                    fill(s, 18)
                    fill(s, 19)
                    if s.G:
                        need(pe, sem("y_sq"), s.nG)
                        need(pe, sem("T_new"), 6 * s.nG)
                        need(pe, sem("rank_used"), s.nR)
                        for j in range(4):
                            mm = pe.matmul(bT[:, 0, :], ones[:], aa[:, j, :], start=(j == 0), stop=(j == 3))
                        mm.then_inc(sem("lnorm_full"), 1)
                    if s.P:
                        need(pe, sem("conv"), 16 * s.pP + 4)
                        need(pe, sem("vn_ready"), s.nG)
                        for j in range(4):
                            mm = pe.matmul(bB[:, j, :], wr_bd[:, j, :], xc[:, j, :], start=True, stop=True)
                        mm.then_inc(sem("gr_full"), 1)
                        need(pe, sem("o_ready"), s.nG)
                        for j in range(4):
                            mm = pe.matmul(bC[:, j, :], wi_bd[:, j, :], xc[:, j, :], start=True, stop=True)
                        mm.then_inc(sem("gi_full"), 1)
                        need(pe, sem("lrs_ln"), s.nG)
                        c = COL["ba"]
                        for k in range(KT):
                            mm = pe.matmul(bTf[:, 0:2 * H], uT[:, k, :], wi[:, k, c:c + 2 * H], start=(k == 0), stop=(k == KT - 1))
                        mm.then_inc(sem("ba_full"), 1)
                    if s.F:
                        need(pe, sem("u_ready"), s.nF)
                        need(pe, sem("h_ready"), s.nO)
                        for k in range(KT):
                            mm = pe.transpose(bO[:, k, :], x_in[:, k:D:KT], ident[:])
                        mm.then_inc(sem("x_turned"), 1)
                steps(pe, body)

            @block.scalar
            def _(act):
                def evac(s, g, name, n):
                    if s.P:
                        need(act, sem(name + "_full"), s.nP)
                        need(act, sem("halo"), 4 * s.pP - 3 + n)
                        nc.scalar.activation(ext[g][:, :, 3:3 + P], pj[n % 2][:], ACT.Copy).then_inc(sem(name + "_evac"), 1)

                def rsqrt(src, dst, scale, bias, ln_sem, out_sem):
                    nc.scalar.activation(dst, src, ACT.Ln, scale=scale, bias=bias).then_inc(sem(ln_sem[0]), 1)
                    need(act, sem(ln_sem[0]), ln_sem[1])
                    nc.scalar.activation(dst, dst, ACT.Exp, scale=-0.5).then_inc(sem(out_sem), 1)

                def body(s):
                    nc.scalar.preload_act_table_set("natural_log_exp_and_others")
                    if s.G:
                        need(act, sem("k_silu"), s.nG)
                        need(act, sem("yt_ready"), s.pG)
                        nc.scalar.activation(rnk[:], ks[:], ACT.Square).then_inc(sem("sq_k"), 1)
                        need(act, sem("q_silu"), s.nG)
                        need(act, sem("S_new"), s.pG)
                        need(act, sem("intra_full"), s.pG)
                        nc.scalar.activation(rnq[:], qs[:], ACT.Square).then_inc(sem("sq_q"), 1)
                        need(act, sem("al_ready"), s.nG)
                        need(act, sem("g_ready"), s.pG)
                        nc.scalar.activation(ga[:], al[:], ACT.Abs).then_inc(sem("g_ln"), 1)
                        need(act, sem("g_ln"), 3 * s.pG + 1)
                        nc.scalar.activation(ga[:], ga[:], ACT.Exp, scale=-1.0).then_inc(sem("g_ln"), 1)
                        need(act, sem("g_ln"), 3 * s.pG + 2)
                        nc.scalar.activation(ga[:], ga[:], ACT.Ln, bias=1.0).then_inc(sem("g_ln"), 1)
                        need(act, sem("nk_full"), s.nG)
                        rsqrt(bB[:], rnk[:], 1.0, eps[:], ("nk_used", s.nG), "rk_ready")
                        need(act, sem("nq_full"), s.nG)
                        rsqrt(bA[:], rnq[:], 1.0, eps[:], ("nq_used", s.nG), "rq_ready")
                        need(act, sem("la_ready"), s.nG)
                        need(act, sem("lnorm_full"), s.pG)
                        nc.scalar.activation(aa[:], la, ACT.Exp).then_inc(sem("a_exp"), 1)
                        need(act, sem("a_exp"), s.nG)
                        need(act, sem("y_sq"), s.pG)
                        nc.scalar.activation(hh[:], aa[:], ACT.Square).then_inc(sem("a_sq"), 1)
                        need(act, sem("cum_full"), s.nG)
                        need(act, sem("S_new"), s.pG)
                        nc.scalar.activation(gl8[:], bTf[:, 0:8], ACT.Copy).then_inc(sem("gl8_ready"), 1)
                        need(act, sem("gl8_ready"), s.nG)
                        nc.scalar.activation(eg8[:], gl8[:], ACT.Exp).then_inc(sem("eg8_ready"), 1)
                        need(act, sem("ekd_raw"), s.nG)
                        nc.scalar.activation(ekd[:], ekd[:], ACT.Exp).then_inc(sem("ekd_ready"), 1)
                        need(act, sem("dec_min"), s.nG)
                        nc.scalar.activation(dec[:], dec[:], ACT.Exp).then_inc(sem("dec_exp"), 1)
                    evac(s, 0, "xb", 0)
                    if s.G:
                        need(act, sem("w_ready"), s.nG)
                        nc.scalar.activation(hh[:], hh[:], ACT.Ln, bias=tiny[:]).then_inc(sem("w_ln"), 1)
                        need(act, sem("w_ln"), s.nG)
                        nc.scalar.activation(hh[:], hh[:], ACT.Exp, scale=0.5).then_inc(sem("ib_ready"), 1)
                        need(act, sem("vt_full"), s.nG)
                        need(act, sem("vn_full"), s.pG)
                        nc.scalar.activation(vt[:], bC[:], ACT.Copy).then_inc(sem("vt_ready"), 1)
                    evac(s, 1, "q", 1)
                    if s.O:
                        need(act, sem("ydT_full"), s.nO)
                        need(act, sem("wo_full"), s.pO)
                        nc.scalar.activation(ydT[:], bT[:], ACT.Copy).then_inc(sem("ydT_ready"), 1)
                    if s.F:
                        need(act, sem("x_in"), 16 * s.nF)
                        need(act, sem("u_ready"), s.pF)
                        nc.scalar.activation(junk[:], x_in[:], ACT.Square, accum_out=xst[:, 0:1]).then_inc(sem("x_ss"), 1)
                        need(act, sem("x_ss"), s.nF)
                        rsqrt(xst[:, 0:1], xst[:, 1:2], 1.0 / D, eps[:], ("x_ln", s.nF), "x_norm")
                    if s.G:
                        need(act, sem("T_full"), 6 * s.pG + 1)
                        need(act, sem("M_raw"), s.nG)
                        need(act, sem("qkT_ready"), s.nG)
                        nc.scalar.activation(T[:], bT[:], ACT.Copy).then_inc(sem("T_new"), 1)
                    evac(s, 2, "k", 2)
                    for l in LEVELS:
                        if s.G:
                            c = 6 * s.pG + l - 1
                            if l == 2:
                                need(act, sem("qS_full"), s.nG)
                            need(act, sem("Y_full"), c)
                            nc.scalar.activation(Y[:], bA[:], ACT.Copy).then_inc(sem("Y_new"), 1)
                            if l < 7:
                                need(act, sem("T_full"), c + 1)
                                nc.scalar.activation(T[:], bT[:], ACT.Copy).then_inc(sem("T_new"), 1)
                        if l == 3:
                            evac(s, 3, "v", 3)
                        if l == 4 and s.R:
                            need(act, sem("top_ready"), s.nR)
                            nc.scalar.activation(eg[:], rg8[:, 0:NG], ACT.Exp, bias=rsm[:, 0:1],
                                                 accum_out=rsm[:, 2:3]).then_inc(sem("exp_ready"), 1)
                            nc.scalar.activation(rsm[:, 3:4], rsm[:, 1:2], ACT.Exp).then_inc(sem("exp_ready"), 1)
                        if l == 4 and s.G:
                            need(act, sem("y_lru"), s.nG)
                            nc.scalar.activation(aa[:], hh[:], ACT.Square).then_inc(sem("y_sq"), 1)
                    if s.G:
                        need(act, sem("lnorm_full"), s.nG)
                        need(act, sem("yl_ready"), s.pG)
                        rsqrt(bT[:, 0, :], lrs[:], 1.0 / LRU, eps[:], ("lrs_ln", s.nG), "lrs_ready")
                        need(act, sem("o_ready"), s.nG)
                        need(act, sem("yt_ready"), s.pG)
                        for h in range(H):
                            a = nc.scalar.activation(junk[:, h * P:h * P + P], ot[:, h, :], ACT.Square, accum_out=oss[:, h:h + 1])
                        a.then_inc(sem("o_ss"), 1)
                        need(act, sem("o_ss"), s.nG)
                        rsqrt(oss[:], ors[:], 1.0 / P, eps[:], ("o_ln", s.nG), "o_norm")
                    if s.O:
                        need(act, sem("h_ready"), s.nO)
                        need(act, sem("lg_ready"), s.nR)
                        nc.scalar.activation(junk[:], ht[:], ACT.Square, accum_out=hst[:, 0:1]).then_inc(sem("h_ss"), 1)
                        need(act, sem("h_ss"), s.nO)
                        rsqrt(hst[:, 0:1], hst[:, 1:2], 1.0 / D, eps[:], ("h_ln", s.nO), "h_norm")
                    if s.P:
                        need(act, sem("gr_full"), s.nP)
                        need(act, sem("a_exp"), s.nG)
                        need(act, sem("rt_full"), s.nR)
                        for j in range(4):
                            a = nc.scalar.activation(la[:, j, :], bB[:, j, :], ACT.Sigmoid, bias=lcol[:, 1, j:j + 1])
                        a.then_inc(sem("r_gate"), 1)
                        need(act, sem("gi_full"), s.nP)
                        need(act, sem("h_scan"), s.nG)
                        for j in range(4):
                            a = nc.scalar.activation(gx[:, j, :], bC[:, j, :], ACT.Sigmoid, bias=lcol[:, 2, j:j + 1])
                        a.then_inc(sem("i_gate"), 1)
                        need(act, sem("gb_full"), s.nP)
                        need(act, sem("y_lru"), s.nG)
                        nc.scalar.activation(gg[:], pj[0][:], ACT.Square).then_inc(sem("gb_sq"), 1)
                        need(act, sem("z_full"), s.nP)
                        need(act, sem("yt_ready"), s.nG)
                        nc.scalar.activation(zg[:], pj[1][:], ACT.Sigmoid).then_inc(sem("z_sig"), 1)
                        need(act, sem("conv"), 16 * s.nP)
                        need(act, sem("Y_full"), 6 * s.nG)
                        for n, (src, tmp) in enumerate(((ks, ML[0]), (qs, ML[1]), (vs, Mt))):
                            nc.scalar.activation(tmp[:], src[:], ACT.Sigmoid).then_inc(sem("qkv_sig"), 1)
                        need(act, sem("ba_full"), s.nP)
                        need(act, sem("beta_ready"), s.nG)
                        nc.scalar.activation(sgb[:], bTf[:, 0:H], ACT.Sigmoid).then_inc(sem("sgb_ready"), 1)
                        need(act, sem("gelu_arg"), 2 * s.nP)
                        nc.scalar.activation(gg[:], gg[:], ACT.Sigmoid, scale=2 * 0.7978845608028654).then_inc(sem("gelu_sig"), 1)
                        need(act, sem("la_ready"), s.nP)
                        need(act, sem("w_ready"), s.nG)
                        nc.scalar.activation(th, la, ACT.Tanh, scale=-1.0).then_inc(sem("th_ready"), 1)
                steps(act, body)

            @block.vector
            def _(dve):
                def conv(s, g, dst):
                    if not s.P:
                        return
                    need(dve, sem(("xb", "q", "k", "v")[g] + "_evac"), s.nP)
                    for tap in range(CW):
                        for j in range(4):
                            w = cvw[:, 4 * g + j, tap:tap + 1]
                            src = ext[g][:, j, tap:tap + P]
                            if tap:
                                a = nc.vector.scalar_tensor_tensor(out=dst[:, j, :], in0=src, scalar=w, in1=dst[:, j, :],
                                                                   op0=ALU.mult, op1=ALU.add)
                            elif g == 0:
                                a = nc.vector.tensor_scalar(dst[:, j, :], src, w, lcol[:, 0, j:j + 1], ALU.mult, ALU.add)
                            else:
                                a = nc.vector.tensor_scalar(dst[:, j, :], src, w, None, ALU.mult)
                        a.then_inc(sem("conv"), 1)
                        dve.wait_ge(sem("conv"), 16 * s.pP + 4 * g + tap + 1)
                    nc.vector.tensor_copy(ext[g][:, :, 0:3], ext[g][:, :, P:P + 3]).then_inc(sem("halo"), 1)

                def link(s, ins, k):
                    ins.then_inc(sem("rt_step"), 1)
                    dve.wait_ge(sem("rt_step"), RSTEPS * s.pR + k)

                def body(s):
                    if s.G:
                        need(dve, sem("g_ln"), 3 * s.nG)
                        need(dve, sem("S_new"), s.pG)
                        need(dve, sem("grow_full"), s.pG)
                        nc.vector.scalar_tensor_tensor(out=g4[:], in0=al[:], scalar=0.0, in1=ga[:], op0=ALU.max,
                                                       op1=ALU.add).then_inc(sem("g_sp"), 1)
                        need(dve, sem("sgb_ready"), s.nG)
                        nc.vector.tensor_copy(beta[:], sgb[:]).then_inc(sem("beta_ready"), 1)
                        need(dve, sem("g_sp"), s.nG)
                        nc.vector.tensor_tensor(g4[:], g4[:], nexp_a[:], ALU.mult).then_inc(sem("g_ready"), 1)
                        need(dve, sem("rk_ready"), s.nG)
                        need(dve, sem("kS_full"), s.pG)
                        nc.vector.tensor_tensor(kh[:], ks[:], rnk[:], ALU.mult).then_inc(sem("kh_ready"), 1)
                        need(dve, sem("rq_ready"), s.nG)
                        need(dve, sem("XU_full"), 6 * s.pG)
                        nc.vector.scalar_tensor_tensor(out=qh[:], in0=qs[:], scalar=P ** -0.5, in1=rnq[:], op0=ALU.mult,
                                                       op1=ALU.mult).then_inc(sem("qh_ready"), 1)
                    if s.G:
                        need(dve, sem("gl8_ready"), s.nG)
                        need(dve, sem("kd_ready"), s.pG)
                        nc.vector.tensor_tensor(ekd[:], gl8[:, 4:8], gl8[:, 0:4], ALU.subtract).then_inc(sem("ekd_raw"), 1)
                        need(dve, sem("eg8_ready"), s.nG)
                        nc.vector.tensor_scalar(neg[:], eg8[:, 0:4], -1.0, None, ALU.mult).then_inc(sem("neg_ready"), 1)
                        need(dve, sem("grow_full"), s.nG)
                        nc.vector.tensor_tensor(dec[:], bC[:], rows(gl8[:, 0:4]), ALU.subtract).then_inc(sem("dec_sub"), 1)
                        need(dve, sem("dec_sub"), s.nG)
                        nc.vector.tensor_scalar(dec[:], dec[:], 0.0, None, ALU.min).then_inc(sem("dec_min"), 1)
                        need(dve, sem("a_sq"), s.nG)
                        need(dve, sem("th_ready"), s.nG)
                        nc.vector.scalar_tensor_tensor(out=hh[:], in0=hh[:], scalar=1.0, in1=th, op0=ALU.add,
                                                       op1=ALU.mult).then_inc(sem("w_ready"), 1)
                    if s.R:
                        need(dve, sem("h_turned"), s.nR)
                        need(dve, sem("rt_full"), s.pR)
                        need(dve, sem("a_exp"), s.nG)
                        need(dve, sem("w_ready"), s.nG)
                        for half in range(2):
                            k = 4 * half
                            a = nc.vector.tensor_tensor(hT[:, k:k + 4, :], bO[:, k:k + 4, :], rows(fg[:, k:k + 4]), ALU.mult)
                        a.then_inc(sem("hT_ready"), 1)
                    if s.P:
                        need(dve, sem("gi_full"), s.pP)
                        need(dve, sem("gx_ready"), s.pP)
                    conv(s, 0, xc)
                    if s.G:
                        need(dve, sem("kt_full"), s.nG)
                        need(dve, sem("ekd_ready"), s.nG)
                        need(dve, sem("Su_full"), s.pG)
                        nc.vector.tensor_tensor(kd[:], bT[:], rows(ekd[:]), ALU.mult).then_inc(sem("kd_ready"), 1)
                        need(dve, sem("kk_full"), s.nG)
                        need(dve, sem("dec_ready"), s.nG)
                        need(dve, sem("ML_ready"), 6 * s.pG)
                        nc.vector.tensor_tensor(Mt[:], bA[:], dec[:], ALU.mult).then_inc(sem("M_raw"), 1)
                        need(dve, sem("qk_full"), s.nG)
                        need(dve, sem("intra_full"), s.pG)
                        nc.vector.tensor_tensor(qkT[:], bB[:], dec[:], ALU.mult).then_inc(sem("qkT_ready"), 1)
                    if s.F:
                        need(dve, sem("x_norm"), s.nF)
                        nc.vector.tensor_scalar(x_in[:], x_in[:], xst[:, 1:2], None, ALU.mult).then_inc(sem("u_ready"), 1)
                    if s.G:
                        need(dve, sem("X_tmp"), s.nG)
                        nc.vector.tensor_tensor(X[:], cols(ident[:]), X[:], ALU.subtract).then_inc(sem("X_first"), 1)
                    conv(s, 1, qs)
                    if s.G:
                        need(dve, sem("kS_full"), s.nG)
                        need(dve, sem("neg_ready"), s.nG)
                        for h in range(H):
                            a = nc.vector.scalar_tensor_tensor(out=vt[:, h, :], in0=bC[:, h, :], scalar=neg[:, h:h + 1],
                                                               in1=vt[:, h, :], op0=ALU.mult, op1=ALU.add)
                        a.then_inc(sem("R_ready"), 1)
                        need(dve, sem("qS_full"), s.nG)
                        nc.vector.tensor_tensor(ot[:], bA[:], rows(eg8[:, 0:4]), ALU.mult).then_inc(sem("o1_ready"), 1)
                        need(dve, sem("b_ready"), s.nG)
                        need(dve, sem("hl_saved"), s.pG)
                        for j in range(4):
                            a = nc.vector.tensor_tensor_scan(out=hh[:, j, :], data0=aa[:, j, :], data1=gx[:, j, :],
                                                             initial=hlast[:, j:j + 1], op0=ALU.mult, op1=ALU.add)
                        a.then_inc(sem("h_scan"), 1)
                        need(dve, sem("h_scan"), s.nG)
                        nc.vector.tensor_copy(hlast[:].unsqueeze(2), hh[:, :, P - 1:P]).then_inc(sem("hl_saved"), 1)
                    if s.R:
                        need(dve, sem("rt_full"), s.nR)
                        need(dve, sem("h_norm"), s.nR)
                        nc.vector.scalar_tensor_tensor(out=lg[:], in0=bTf[:, 0:NG + NE], scalar=hst[:, 1:2], in1=rb[:],
                                                       op0=ALU.mult, op1=ALU.add).then_inc(sem("lg_ready"), 1)
                    for l in LEVELS:
                        if s.G:
                            c = 6 * s.pG + l - 1
                            need(dve, sem("XU_full"), c)
                            need(dve, sem("T_full"), c)
                            nc.vector.tensor_tensor(X[:], X[:], bB[:], ALU.subtract).then_inc(sem("X_new"), 1)
                        if l == 2:
                            conv(s, 2, ks)
                        if l == 3 and s.R:
                            need(dve, sem("lg_ready"), s.nR)
                            link(s, nc.vector.tensor_copy(rg8[:, 0:NG], lg[:, 0:NG]), 1)
                            settle(dve)
                            link(s, nc.vector.max(m8[:], rg8[:]), 2)
                            settle(dve)
                            link(s, nc.vector.max_index(i8[:], m8[:], rg8[:]), 3)
                            nc.vector.tensor_scalar(rsm[:, 0:1], m8[:, 0:1], -1.0, None, ALU.mult)
                            link(s, nc.vector.tensor_copy(rsm[:, 4:5], i8[:, 0:1]), 4)
                            nc.vector.tensor_scalar(rsm[:, 5:6], rsm[:, 4:5], float(EPG), None, ALU.mult)
                            link(s, nc.vector.tensor_scalar(ohg[:], iota_e[:, 0:NG], rsm[:, 4:5], None, ALU.is_equal), 5)
                            link(s, nc.vector.tensor_tensor(elg[:], lg[:, NG:].rearrange("p (g e) -> p e g", g=NG),
                                                            ohg[:].unsqueeze(1).to_broadcast([P, EPG, NG]), ALU.mult), 6)
                            link(s, nc.vector.tensor_reduce(el8[:], elg[:], AX, ALU.add), 7)
                            settle(dve)
                            link(s, nc.vector.max(v8[:], el8[:]), 8)
                            nc.vector.tensor_tensor(rsm[:, 1:2], v8[:, 1:2], v8[:, 0:1], ALU.subtract).then_inc(sem("top_ready"), 1)
                            settle(dve)
                            link(s, nc.vector.max_index(j8[:], v8[:], el8[:]), 9)
                            link(s, nc.vector.tensor_copy(rsm[:, 6:8], j8[:, 0:2]), 10)
                            need(dve, sem("saved_ready"), s.pR)
                            link(s, nc.vector.tensor_scalar(rt6[:, 0:2], rsm[:, 6:8], rsm[:, 5:6], None, ALU.add), 11)
                            need(dve, sem("rank_full"), s.pR)
                            for a in range(2):
                                ins = nc.vector.tensor_scalar(oh[:, a, :], iota_e[:], rt6[:, a:a + 1], None, ALU.is_equal)
                            link(s, ins, 12)
                            nc.vector.tensor_tensor(ohs[:], oh[:, 0, :], oh[:, 1, :], ALU.add).then_inc(sem("oh_ready"), 1)
                        if l == 5:
                            conv(s, 3, vs)
                            if s.R:
                                need(dve, sem("rank_full"), s.nR)
                                link(s, nc.vector.tensor_tensor(pre[:], bTf[:, 0:NE], cnt[:], ALU.add), 13)
                                nc.vector.tensor_tensor(cnt[:], cnt[:], bTf[:, NE:2 * NE], ALU.add).then_inc(sem("rank_used"), 1)
                                need(dve, sem("rank_used"), s.nR)
                    if s.G:
                        need(dve, sem("vn_full"), s.nG)
                        nc.vector.tensor_tensor(vn[:], bB[:], rows(beta[:]), ALU.mult).then_inc(sem("vn_ready"), 1)
                    if s.R:
                        for a in range(2):
                            ins = nc.vector.tensor_tensor_reduce(jr[:], oh[:, a, :], pre[:], 1.0, 0.0, ALU.mult, ALU.add,
                                                                 rt6[:, 2 + a:3 + a])
                            link(s, ins, 14 + a)
                        need(dve, sem("scattered"), 32 * s.pR)
                        nc.vector.scalar_tensor_tensor(out=posf[:], in0=rt6[:, 0:2], scalar=float(TCAP), in1=rt6[:, 2:4],
                                                       op0=ALU.mult, op1=ALU.add)
                        link(s, nc.vector.tensor_copy(toki[:], tokf[:]), 16)
                        link(s, nc.vector.tensor_scalar(tokf[:], tokf[:], float(P), None, ALU.add), 17)
                        nc.vector.tensor_copy(posi[:], posf[:]).then_inc(sem("pos_ready"), 1)
                        need(dve, sem("exp_ready"), 2 * s.nR)
                        link(s, nc.vector.scalar_tensor_tensor(out=rsm[:, 8:9], in0=rsm[:, 3:4], scalar=1.0, in1=rsm[:, 2:3],
                                                               op0=ALU.add, op1=ALU.mult), 18)
                        link(s, nc.vector.reciprocal(rt6[:, 4:5], rsm[:, 8:9]), 19)
                        link(s, nc.vector.tensor_tensor(rt6[:, 5:6], rt6[:, 4:5], rsm[:, 3:4], ALU.mult), 20)
                        nc.vector.tensor_copy(saved[:, bass.ds(s.pR, 1), :], rt6[:].unsqueeze(1)).then_inc(sem("saved_ready"), 1)
                    if s.G:
                        need(dve, sem("Su_full"), s.nG)
                        for h in range(H):
                            a = nc.vector.scalar_tensor_tensor(out=St[:, h, :], in0=St[:, h, :], scalar=eg8[:, 4 + h:5 + h],
                                                               in1=bA[:, h, :], op0=ALU.mult, op1=ALU.add)
                        a.then_inc(sem("S_new"), 1)
                        need(dve, sem("intra_full"), s.nG)
                        nc.vector.tensor_tensor(ot[:], ot[:], bC[:], ALU.add).then_inc(sem("o_ready"), 1)
                    if s.O:
                        need(dve, sem("wo_full"), s.nO)
                        need(dve, sem("x_res"), 16 * s.nO)
                        for half in range(2):
                            c = slice(512 * half, 512 * half + 512)
                            a = nc.vector.tensor_tensor(ht[:, c], ht[:, c], bOf[:, c], ALU.add)
                        a.then_inc(sem("h_ready"), 1)
                    if s.G:
                        need(dve, sem("lrs_ready"), s.nG)
                        need(dve, sem("wo_full"), s.nO)
                        for j in range(4):
                            a = nc.vector.scalar_tensor_tensor(out=yl[:, j, :], in0=hh[:, j, :], scalar=lcol[:, 4, j:j + 1],
                                                               in1=lrs[:], op0=ALU.mult, op1=ALU.mult)
                        a.then_inc(sem("yl_ready"), 1)
                        need(dve, sem("o_norm"), s.nG)
                        need(dve, sem("zg_ready"), s.nG)
                        need(dve, sem("ydT_full"), s.nO)
                        for h in range(H):
                            a = nc.vector.scalar_tensor_tensor(out=yt[:, h, :], in0=ot[:, h, :], scalar=ors[:, h:h + 1],
                                                               in1=zg[:, h, :], op0=ALU.mult, op1=ALU.mult)
                        a.then_inc(sem("yt_ready"), 1)
                    if s.P:
                        need(dve, sem("gb_sq"), s.nP)
                        nc.vector.tensor_scalar(gg[:], gg[:], 0.044715, 1.0, ALU.mult, ALU.add).then_inc(sem("gelu_arg"), 1)
                        need(dve, sem("gelu_arg"), 2 * s.pP + 1)
                        nc.vector.tensor_tensor(gg[:], gg[:], pj[0][:], ALU.mult).then_inc(sem("gelu_arg"), 1)
                        need(dve, sem("z_sig"), s.nP)
                        nc.vector.tensor_tensor(zg[:], zg[:], pj[1][:], ALU.mult).then_inc(sem("z_used"), 1)
                        need(dve, sem("qkv_sig"), 3 * s.pP + 1)
                        nc.vector.tensor_tensor(ks[:], ks[:], ML[0][:], ALU.mult).then_inc(sem("k_silu"), 1)
                        need(dve, sem("qkv_sig"), 3 * s.pP + 2)
                        nc.vector.tensor_tensor(qs[:], qs[:], ML[1][:], ALU.mult).then_inc(sem("q_silu"), 1)
                        need(dve, sem("ba_full"), s.nP)
                        need(dve, sem("g_ready"), s.nG)
                        need(dve, sem("sgb_ready"), s.nP)
                        nc.vector.tensor_tensor(al[:], bTf[:, H:2 * H], dt_b[:], ALU.add).then_inc(sem("al_ready"), 1)
                        need(dve, sem("qkv_sig"), 3 * s.nP)
                        nc.vector.tensor_tensor(vs[:], vs[:], Mt[:], ALU.mult).then_inc(sem("v_silu"), 1)
                        need(dve, sem("gelu_sig"), s.nP)
                        nc.vector.tensor_tensor(gg[:], gg[:], pj[0][:], ALU.mult).then_inc(sem("gb_used"), 1)
                    if s.F:
                        need(dve, sem("x_turned"), s.nF)
                        need(dve, sem("ba_full"), s.nP)
                        for half in range(2):
                            k = 4 * half
                            a = nc.vector.tensor_tensor(uT[:, k:k + 4, :], bO[:, k:k + 4, :], rows(mg[:, k:k + 4]), ALU.mult)
                        a.then_inc(sem("uT_ready"), 1)
                steps(dve, body)
                need(dve, sem("saved_ready"), TILES - 1)
                need(dve, sem("rank_used"), TILES - 1)

            @block.gpsimd
            def _(pool):
                def body(s):
                    if s.G:
                        need(pool, sem("g_ready"), s.nG)
                        need(pool, sem("Y_full"), 6 * s.pG)
                        nc.gpsimd.tensor_tensor(dec[:], cols(tri[:]), rows(g4[:]), ALU.mult).then_inc(sem("gtri_ready"), 1)
                        need(pool, sem("dec_exp"), s.nG)
                        nc.gpsimd.tensor_tensor(dec[:], dec[:], cols(tri[:]), ALU.mult).then_inc(sem("dec_ready"), 1)
                        need(pool, sem("M_raw"), s.nG)
                        need(pool, sem("beta_ready"), s.nG)
                        nc.gpsimd.tensor_tensor(Mt[:], Mt[:], rows(beta[:]), ALU.mult).then_inc(sem("M_ready"), 1)
                        need(pool, sem("M_ready"), s.nG)
                        need(pool, sem("vn_full"), s.pG)
                        nc.gpsimd.tensor_tensor(X[:], Mt[:], cols(lvl[:, 0, :]), ALU.mult).then_inc(sem("X_tmp"), 1)
                        need(pool, sem("ib_ready"), s.nG)
                        need(pool, sem("gx_ready"), s.nG)
                        b = nc.gpsimd.tensor_tensor(gx[:], gx[:], hh[:], ALU.mult)
                        if isinstance(s.i, int) and s.i == 0:
                            b.then_inc(sem("b_raw"), 1)
                            pool.wait_ge(sem("b_raw"), 1)
                            b = nc.gpsimd.memset(gx[:, :, 0:PAD], 0.0)
                        b.then_inc(sem("b_ready"), 1)
                    for l in LEVELS:
                        if s.G:
                            if l < 4:
                                need(pool, sem("k_silu"), s.pP)
                                need(pool, sem("q_silu"), s.pP)
                            else:
                                need(pool, sem("Y_full"), 6 * s.pG + l - 3)
                            nc.gpsimd.tensor_tensor(ML[l % 2][:], Mt[:], cols(lvl[:, l - 1, :]), ALU.mult).then_inc(sem("ML_ready"), 1)
                        if l == 4 and s.G:
                            need(pool, sem("hl_saved"), s.nG)
                            need(pool, sem("gb_used"), s.nG)
                            nc.gpsimd.tensor_tensor(hh[:], hh[:], gg[:], ALU.mult).then_inc(sem("y_lru"), 1)
                    if s.R:
                        need(pool, sem("pos_ready"), s.nR)
                        settle(pool)
                        for a in range(2):
                            pool.indirect_dma_start(out=idx_tab, out_offset=bass.IndirectOffsetOnAxis(ap=posi[:, a:a + 1], axis=0),
                                                    in_=toki[:], in_offset=None).then_inc(sem("scattered"), 16)
                    if s.P:
                        need(pool, sem("r_gate"), s.nP)
                        nc.gpsimd.tensor_tensor(la, la, rows(cl[:]), ALU.mult).then_inc(sem("la_ready"), 1)
                        need(pool, sem("i_gate"), s.nP)
                        nc.gpsimd.tensor_tensor(gx[:], gx[:], xc[:], ALU.mult).then_inc(sem("gx_ready"), 1)
                        need(pool, sem("z_used"), s.nP)
                        nc.gpsimd.tensor_tensor(zg[:], zg[:], cols(dng[:]), ALU.mult).then_inc(sem("zg_ready"), 1)
                steps(pool, body)
                need(pool, sem("scattered"), 32 * (TILES - 1))

        free = WSLOTS * SLOT + 2 * D
        room = W[:, free + 3 * FE:free + 3 * FE + 6 * NE].rearrange("p (n e) -> p n e", n=6)
        nb, end, start, ohb = (room[:, n, :] for n in range(4))
        ti, endi = (room[:, n, :].bitcast(I32) for n in (4, 5))
        tcol = sb("tcol", [P, 8])
        tcoli = sb("tcoli", [P, 4], I32)
        blk = W[0:1, free + 3 * FE + 6 * NE:free + 3 * FE + 6 * NE + 3 * P].bitcast(I32)
        dstf = sb("dstf", [P, 2, SEQ // P])
        dsti = sb("dsti", [P, 2, SEQ // P], I32)
        big = x_in[:].rearrange("p (t e) -> p t e", e=NE)
        NT = SEQ // P

        with nc.Block() as block:
            @block.vector
            def _(dve):
                done = [0]

                def link(ins):
                    done[0] += 1
                    ins.then_inc(sem("tab_step"), 1)
                    dve.wait_ge(sem("tab_step"), done[0])

                link(nc.vector.tensor_scalar(nb, cnt[:], 1.0 / P, (P - 1.0) / P - 0.5 + 0.5 / P, ALU.mult, ALU.add))
                link(nc.vector.tensor_copy(ti, nb))
                link(nc.vector.tensor_copy(nb, ti))
                link(nc.vector.memset(start, 0.0))
                link(nc.vector.tensor_tensor_scan(out=end[:], data0=nb[:], data1=start[:], initial=0.0, op0=ALU.add, op1=ALU.add))
                link(nc.vector.tensor_tensor(start, end, nb, ALU.subtract))
                nc.vector.tensor_scalar(endi, end, 1.0, None, ALU.add).then_inc(sem("end_ready"), 1)
                link(nc.vector.tensor_scalar(ohb, end, iota_p[:], None, ALU.is_le))
                link(nc.vector.tensor_reduce(tcol[:, 0:1], ohb, AX, ALU.add))
                link(nc.vector.tensor_scalar(tcol[:, 0:1], tcol[:, 0:1], NE - 1.0, None, ALU.min))
                link(nc.vector.tensor_scalar(ohb, iota_e[:], tcol[:, 0:1], None, ALU.is_equal))
                link(nc.vector.tensor_tensor_reduce(nb, ohb, start, 1.0, 0.0, ALU.mult, ALU.add, tcol[:, 1:2]))
                link(nc.vector.tensor_tensor(tcol[:, 1:2], iota_p[:], tcol[:, 1:2], ALU.subtract))
                link(nc.vector.tensor_scalar(tcol[:, 1:2], tcol[:, 1:2], TCAP // P - 1.0, float(P), ALU.min, ALU.mult))
                link(nc.vector.scalar_tensor_tensor(out=tcol[:, 4:5], in0=tcol[:, 0:1], scalar=float(TCAP), in1=tcol[:, 1:2],
                                                    op0=ALU.mult, op1=ALU.add))
                link(nc.vector.tensor_scalar(tcol[:, 2:3], tcol[:, 0:1], 1.0, None, ALU.add))
                link(nc.vector.tensor_scalar(tcol[:, 5:6], tcol[:, 0:1], 1.0 / WSLOTS, 0.5 / WSLOTS - 0.5, ALU.mult, ALU.add))
                link(nc.vector.tensor_copy(tcoli[:, 0:1], tcol[:, 5:6]))
                link(nc.vector.tensor_copy(tcol[:, 5:6], tcoli[:, 0:1]))
                link(nc.vector.scalar_tensor_tensor(out=tcol[:, 3:4], in0=tcol[:, 5:6], scalar=-float(WSLOTS), in1=tcol[:, 0:1],
                                                    op0=ALU.mult, op1=ALU.add))
                link(nc.vector.tensor_scalar(tcol[:, 3:4], tcol[:, 3:4], float(SLOT), None, ALU.mult))
                nc.vector.tensor_copy(tcoli[:, 0:3], tcol[:, 2:5]).then_inc(sem("blk_ready"), 1)
                for a in range(2):
                    link(nc.vector.tensor_tensor(big, iota_e[:].unsqueeze(1).to_broadcast([P, NT, NE]),
                                                 saved[:, :, a:a + 1].to_broadcast([P, NT, NE]), ALU.is_equal))
                    link(nc.vector.tensor_tensor(big, big, start.unsqueeze(1).to_broadcast([P, NT, NE]), ALU.mult))
                    link(nc.vector.tensor_reduce(dstf[:, a, :], big, AX, ALU.add))
                    link(nc.vector.scalar_tensor_tensor(out=dstf[:, a, :], in0=dstf[:, a, :], scalar=float(P),
                                                        in1=saved[:, :, 2 + a], op0=ALU.mult, op1=ALU.add))
                link(nc.vector.tensor_copy(dsti[:], dstf[:]))

            @block.sync
            def _(sp):
                sp.wait_ge(sem("blk_ready"), 1)
                sp.dma_start(blk_tab, tcoli[:, 0:3]).then_inc(sem("blk_out"), 16)
                sp.wait_ge(sem("blk_out"), 16)
                sp.dma_start(blk, blk_tab.rearrange("p c -> (p c)").unsqueeze(0)).then_inc(sem("blk_in"), 16)
                sp.wait_ge(sem("blk_in"), 16)
                sp.wait_ge(sem("end_ready"), 1)

        retire(keep=("idx_zeroed", "scattered"))
        xg = (x_in, ht)
        xT = uT
        hm = W[:, free:free + FE]
        sm = W[:, free + FE:free + 2 * FE]
        hm2 = W[:, free + 2 * FE:free + 3 * FE].rearrange("p (j n) -> p j n", j=2)
        gst = sb("gst", [P, 2, 3])
        yo = (W[:, WSLOTS * SLOT:WSLOTS * SLOT + D], W[:, WSLOTS * SLOT + D:WSLOTS * SLOT + 2 * D])
        gid = [sb(f"gid{n}", [P, 1], I32) for n in range(2)]

        def blocks(eng, body):
            pairs = (NBLK - 2) // 2
            for b in range(3):
                body(b, b % 2)
            with eng.Fori(1, pairs) as p:
                body(1 + 2 * p, 1)
                body(2 + 2 * p, 0)
            for b in range(1 + 2 * pairs, NBLK):
                body(b, b % 2)

        with nc.Block() as block:
            @block.sync
            def _(sp):
                def load(e, slot):
                    o = slot * SLOT
                    sp.dma_start(W[:, o:o + KT * FE], w_gate[bass.ds(e, 1)].rearrange("o (p k) f -> p (o k f)", k=KT)
                                 ).then_inc(sem(f"w_loaded{slot}"), 16)
                    sp.dma_start(W[:, o + KT * FE:o + GU], w_up[bass.ds(e, 1)].rearrange("o (p k) f -> p (o k f)", k=KT)
                                 ).then_inc(sem(f"w_loaded{slot}"), 16)
                    sp.dma_start(W[:, o + GU:o + SLOT], w_down[bass.ds(e, 1)].rearrange("o (p j) n -> p (o j n)", j=2)
                                 ).then_inc(sem(f"w_loaded{slot}"), 16)

                for slot in range(WSLOTS):
                    load(slot, slot)
                for slot in range(WSLOTS - 1):
                    sp.wait_ge(sem(f"w_loaded{slot}"), 48)
                    sp.sem_inc(sem("w_ready"), 1)
                with sp.Fori(1, NE // WSLOTS) as q:
                    for slot in range(WSLOTS):
                        prev = (slot - 1) % WSLOTS
                        sp.wait_ge(sem(f"w_loaded{prev}"), 48 * q + (48 if slot else 0))
                        sp.sem_inc(sem("w_ready"), 1)
                        last = sp.value_load(endi[0:1, bass.ds((q - 1) * WSLOTS + slot, 1)], min_val=1, max_val=NBLK + 1)
                        sp.wait_ge(sem("y_full"), last)
                        settle(sp)
                        load(q * WSLOTS + slot, slot)
                sp.wait_ge(sem(f"w_loaded{WSLOTS - 1}"), 48 * (NE // WSLOTS))
                sp.sem_inc(sem("w_ready"), 1)

            @block.gpsimd
            def _(pool):
                def body(b, par):
                    off = pool.value_load(blk[0:1, bass.ds(3 * b + 2, 1)], min_val=0, max_val=(NE - 1) * TCAP + TCAP - P)
                    pool.dma_start(gid[par][:], idx_tab[bass.ds(off, P), :]).then_inc(sem("gid_in"), 16)
                    pool.wait_ge(sem("gid_in"), 16 * (b + 1))
                    need(pool, sem("xg_turned"), b - 1)
                    need(pool, sem("g_norm"), b - 1)
                    settle(pool)
                    pool.indirect_dma_start(out=xg[par][:], out_offset=None, in_=h_rows,
                                            in_offset=bass.IndirectOffsetOnAxis(ap=gid[par][:], axis=0)
                                            ).then_inc(sem(f"xg_in{par}"), 16)
                    pool.wait_ge(sem(f"xg_in{par}"), 16 * (b // 2 + 1) if isinstance(b, int) else xg_count(b, par))
                    pool.sem_inc(sem("xg_ready"), 1)

                def xg_count(b, par):
                    return 8 * b + (16 if par == 0 else 8)
                blocks(pool, body)

            @block.tensor
            def _(pe):
                def slot_of(b):
                    return pe.value_load(blk[0:1, bass.ds(3 * b + 1, 1)], min_val=0, max_val=(WSLOTS - 1) * SLOT)

                def turn_x(b, par):
                    pe.wait_ge(sem("xg_ready"), b + 1)
                    need(pe, sem("xT_ready"), b)
                    for k in range(KT):
                        mm = pe.transpose(bO[:, k, :], xg[par][:, k:D:KT], ident[:])
                    mm.then_inc(sem("xg_turned"), 1)

                def down(b):
                    w = W[:, bass.ds(slot_of(b) + GU, WD)].rearrange("p (j n) -> p j n", j=2)
                    pe.wait_ge(sem("hm2_ready"), b + 1)
                    need(pe, sem("yo_a"), b)
                    need(pe, sem("yo_b"), b)
                    for half in range(2):
                        for j in range(2):
                            mm = pe.matmul(flat(pj[half]), hm2[:, j, :], w[:, j, 512 * half:512 * half + 512],
                                           start=(j == 0), stop=(j == 1))
                    mm.then_inc(sem("y_full"), 1)

                def body(b, par):
                    if isinstance(b, int) and b == 0:
                        turn_x(0, 0)
                    e1 = pe.value_load(blk[0:1, bass.ds(3 * b, 1)], min_val=1, max_val=NE)
                    w = W[:, bass.ds(slot_of(b), GU)].rearrange("p (g k f) -> p k g f", g=2, k=KT)
                    pe.wait_ge(sem("w_ready"), e1)
                    pe.wait_ge(sem("xT_ready"), b + 1)
                    need(pe, sem("hm_ready"), b)
                    for k in range(KT):
                        mm = pe.matmul(bA[:].rearrange("p a b -> p (a b)").rearrange("p (g f) -> p g f", g=2), xT[:, k, :],
                                       w[:, k], start=(k == 0), stop=(k == KT - 1))
                    mm.then_inc(sem("gu_full"), 1)
                    if not (isinstance(b, int) and b == NBLK - 1):
                        turn_x(b + 1, 1 - par)
                    if not (isinstance(b, int) and b == 0):
                        down(b - 1)
                    pe.wait_ge(sem("hm_ready"), b + 1)
                    need(pe, sem("hm2_ready"), b)
                    for j in range(2):
                        mm = pe.transpose(bT[:, j, :], hm[:, j:FE:2], ident[:])
                    mm.then_inc(sem("hm_turned"), 1)
                    if isinstance(b, int) and b == NBLK - 1:
                        down(b)
                pe.sem_inc(sem("y_full"), 1)
                blocks(pe, body)

            @block.scalar
            def _(act):
                nc.scalar.preload_act_table_set("natural_log_exp_and_others")

                def norm(b, par):
                    act.wait_ge(sem("xg_ready"), b + 1)
                    need(act, sem("hm_ready"), b - 1)
                    nc.scalar.activation(junk[:], xg[par][:], ACT.Square, accum_out=gst[:, par, 0:1]).then_inc(sem("g_ss"), 1)
                    act.wait_ge(sem("g_ss"), b + 1)
                    nc.scalar.activation(gst[:, par, 1:2], gst[:, par, 0:1], ACT.Ln, scale=1.0 / D, bias=eps[:]).then_inc(sem("g_ln2"), 1)
                    act.wait_ge(sem("g_ln2"), b + 1)
                    nc.scalar.activation(gst[:, par, 1:2], gst[:, par, 1:2], ACT.Exp, scale=-0.5).then_inc(sem("g_norm"), 1)
                    act.wait_ge(sem("g_norm"), b + 1)
                    nc.scalar.activation(gst[:, par, 2:3], gst[:, par, 1:2], ACT.Copy, scale=-1.0).then_inc(sem("g_neg"), 1)

                def out_half(b, par):
                    act.wait_ge(sem("y_full"), b + 2)
                    yo_free(b, par)
                    nc.scalar.activation(yo[par][:, 0:512], flat(pj[0]), ACT.Copy).then_inc(sem("yo_a"), 1)
                    act.wait_ge(sem("yo_a"), b + 1)
                    act.wait_ge(sem("yo_b"), b + 1)
                    act.dma_start(y_rows[bass.ds(b * P, P), :], yo[par]).then_inc(sem(f"y_stored{par}"), 16)

                def yo_free(b, par):
                    need(act, sem(f"y_stored{par}"), 8 * b - (8 if par else 0))

                def body(b, par):
                    if isinstance(b, int) and b == 0:
                        norm(0, 0)
                    act.wait_ge(sem("gu_full"), b + 1)
                    act.wait_ge(sem("g_neg"), b + 1)
                    need(act, sem("hm_ready"), b)
                    nc.scalar.activation(sm, flat(bA)[:, 0:FE], ACT.Exp, scale=gst[:, par, 2:3]).then_inc(sem("silu_exp"), 1)
                    if not (isinstance(b, int) and b == NBLK - 1):
                        norm(b + 1, 1 - par)
                    if not (isinstance(b, int) and b == 0):
                        out_half(b - 1, 1 - par)
                    act.wait_ge(sem("hm_turned"), b + 1)
                    need(act, sem("y_full"), b + 1)
                    nc.scalar.activation(hm2, bT[:, 0:2, :], ACT.Copy).then_inc(sem("hm2_ready"), 1)
                    if isinstance(b, int) and b == NBLK - 1:
                        out_half(b, par)
                blocks(act, body)
                act.wait_ge(sem("y_stored0"), 16 * ((NBLK + 1) // 2))
                act.wait_ge(sem("y_stored1"), 16 * (NBLK // 2))

            @block.vector
            def _(dve):
                def turned(b):
                    dve.wait_ge(sem("xg_turned"), b + 1)
                    need(dve, sem("gu_full"), b)
                    for half in range(2):
                        k = 4 * half
                        a = nc.vector.tensor_tensor(xT[:, k:k + 4, :], bO[:, k:k + 4, :], rows(fg[:, k:k + 4]), ALU.mult)
                    a.then_inc(sem("xT_ready"), 1)

                def out_half(b, par):
                    dve.wait_ge(sem("y_full"), b + 2)
                    need(dve, sem(f"y_stored{par}"), 8 * b - (8 if par else 0))
                    nc.vector.tensor_copy(yo[par][:, 512:D], flat(pj[1])).then_inc(sem("yo_b"), 1)

                def body(b, par):
                    if isinstance(b, int) and b == 0:
                        turned(0)
                    rs = gst[:, par, 1:2]
                    dve.wait_ge(sem("silu_exp"), b + 1)
                    nc.vector.tensor_scalar(sm, sm, 1.0, None, ALU.add).then_inc(sem("silu"), 1)
                    dve.wait_ge(sem("silu"), 3 * b + 1)
                    nc.vector.reciprocal(sm, sm).then_inc(sem("silu"), 1)
                    dve.wait_ge(sem("silu"), 3 * b + 2)
                    nc.vector.scalar_tensor_tensor(out=sm, in0=flat(bA)[:, 0:FE], scalar=rs, in1=sm, op0=ALU.mult,
                                                   op1=ALU.mult).then_inc(sem("silu"), 1)
                    dve.wait_ge(sem("silu"), 3 * b + 3)
                    need(dve, sem("hm_turned"), b)
                    nc.vector.scalar_tensor_tensor(out=hm, in0=flat(bA)[:, FE:2 * FE], scalar=rs, in1=sm, op0=ALU.mult,
                                                   op1=ALU.mult).then_inc(sem("hm_ready"), 1)
                    if not (isinstance(b, int) and b == NBLK - 1):
                        turned(b + 1)
                    if not (isinstance(b, int) and b == 0):
                        out_half(b - 1, 1 - par)
                    if isinstance(b, int) and b == NBLK - 1:
                        out_half(b, par)
                blocks(dve, body)

        fgr = W[:, 0:D]
        ya = [W[:, (1 + n) * D:(2 + n) * D] for n in range(2)]
        yb = [W[:, (3 + n) * D:(4 + n) * D] for n in range(2)]
        hb = [W[:, (5 + n) * D:(6 + n) * D] for n in range(2)]
        fo = [W[:, (7 + n) * D:(8 + n) * D] for n in range(2)]
        di = [[sb(f"di{n}{a}", [P, 1], I32) for a in range(2)] for n in range(2)]
        g2 = [sb(f"g2{n}", [P, 2]) for n in range(2)]
        fst = sb("fst", [P, 2, 2])

        def pairs(eng, body):
            for par in range(2):
                body(0, par, par)
            with eng.Fori(1, NT // 2) as p:
                for par in range(2):
                    body(p, 2 * p + par, par)

        with nc.Block() as block:
            @block.sync
            def _(sp):
                sp.dma_start(fgr, final_g.partition_broadcast(P)).then_inc(sem("fg_in"), 16)

                def body(p, t, par):
                    need(sp, sem(f"h_used{par}"), p)
                    settle(sp)
                    sp.dma_start(hb[par], h_rows[bass.ds(t * P, P), :]).then_inc(sem(f"h_in{par}"), 16)
                pairs(sp, body)

            @block.gpsimd
            def _(pool):
                def body(p, t, par):
                    pool.wait_ge(sem("di_ready"), t + 1)
                    need(pool, sem(f"y_used{par}"), p)
                    settle(pool)
                    for a, y in enumerate((ya, yb)):
                        pool.indirect_dma_start(out=y[par], out_offset=None, in_=y_rows,
                                                in_offset=bass.IndirectOffsetOnAxis(ap=di[par][a][:], axis=0)
                                                ).then_inc(sem(f"y{a}_in{par}"), 16)
                pairs(pool, body)

            @block.scalar
            def _(act):
                def body(p, t, par):
                    need(act, sem(f"y0_in{par}"), 16 * p)
                    need(act, sem(f"y1_in{par}"), 16 * p)
                    for a in range(2):
                        c = nc.scalar.copy(di[par][a][:], dsti[:, a, bass.ds(t, 1)])
                    c.then_inc(sem("di_ready"), 1)
                    need(act, sem(f"y_used{par}"), p)
                    nc.scalar.copy(g2[par][:].unsqueeze(1), saved[:, bass.ds(t, 1), 4:6]).then_inc(sem("g2_ready"), 1)
                    act.wait_ge(sem("h2_ready"), t + 1)
                    need(act, sem(f"fo_ready{par}"), p)
                    nc.scalar.activation(junk[:], hb[par], ACT.Square, accum_out=fst[:, par, 0:1]).then_inc(sem("f_ss"), 1)
                    act.wait_ge(sem("f_ss"), t + 1)
                    nc.scalar.activation(fst[:, par, 1:2], fst[:, par, 0:1], ACT.Ln, scale=1.0 / D, bias=eps[:]).then_inc(sem("f_ln"), 1)
                    act.wait_ge(sem("f_ln"), t + 1)
                    nc.scalar.activation(fst[:, par, 1:2], fst[:, par, 1:2], ACT.Exp, scale=-0.5).then_inc(sem("f_norm"), 1)
                    act.wait_ge(sem(f"fo_ready{par}"), p + 1)
                    act.dma_start(out[bass.ds(t * P, P), :], fo[par]).then_inc(sem(f"out{par}"), 16)
                pairs(act, body)
                act.wait_ge(sem("out0"), 16 * (NT // 2))
                act.wait_ge(sem("out1"), 16 * (NT // 2))

            @block.vector
            def _(dve):
                dve.wait_ge(sem("fg_in"), 16)

                def body(p, t, par):
                    dve.wait_ge(sem(f"h_in{par}"), 16 * (p + 1))
                    dve.wait_ge(sem(f"y0_in{par}"), 16 * (p + 1))
                    dve.wait_ge(sem("g2_ready"), t + 1)
                    nc.vector.scalar_tensor_tensor(out=ya[par], in0=ya[par], scalar=g2[par][:, 0:1], in1=hb[par], op0=ALU.mult,
                                                   op1=ALU.add).then_inc(sem("h1_sum"), 1)
                    dve.wait_ge(sem("h1_sum"), t + 1)
                    dve.wait_ge(sem(f"y1_in{par}"), 16 * (p + 1))
                    nc.vector.scalar_tensor_tensor(out=hb[par], in0=yb[par], scalar=g2[par][:, 1:2], in1=ya[par], op0=ALU.mult,
                                                   op1=ALU.add).then_inc(sem("h2_ready"), 1)
                    dve.wait_ge(sem("h2_ready"), t + 1)
                    dve.sem_inc(sem(f"y_used{par}"), 1)
                    dve.wait_ge(sem("f_norm"), t + 1)
                    need(dve, sem(f"out{par}"), 16 * p)
                    nc.vector.scalar_tensor_tensor(out=fo[par], in0=hb[par], scalar=fst[:, par, 1:2], in1=fgr, op0=ALU.mult,
                                                   op1=ALU.mult).then_inc(sem(f"fo_ready{par}"), 1)
                    dve.wait_ge(sem(f"fo_ready{par}"), p + 1)
                    dve.sem_inc(sem(f"h_used{par}"), 1)
                pairs(dve, body)


def kernel(**inputs):
    import numpy as np
    import concourse.bacc as bacc
    from concourse.bass_utils import run_bass_kernel_spmd

    a = {k: np.asarray(v) for k, v in inputs.items()}
    f32 = np.float32
    x = a["x"][0]

    def tiled(v):
        return v.reshape(-1, P).T

    arrays = {
        "xm": np.concatenate([np.zeros((PAD, D), x.dtype), a["meta_tokens"], x], axis=0),
        "w_in": a["w_in"][0],
        "w_out": a["w_out"][0],
        "conv_w": np.concatenate([a["lru_conv_w"][0], a["dn_conv_w"][0]], axis=1).reshape(CW, 16, P).transpose(2, 1, 0),
        "lru_cols": np.stack([tiled(a[n][0]) for n in ("lru_conv_b", "lru_b_r", "lru_b_i", "lru_lambda", "lru_out_norm")], axis=1),
        "w_r": a["lru_w_r"][0],
        "w_i": a["lru_w_i"][0],
        "mix_g": a["mix_norm"][0].reshape(P, KT),
        "ffn_g": a["ffn_norm"][0].reshape(P, KT),
        "final_g": a["final_norm"],
        "dn_g": a["dn_out_norm"][0],
        "dn_a": a["dn_a_log"][0],
        "dn_dt": a["dn_dt_bias"][0],
        "w_router": np.concatenate([a["router_group_w"][0], a["router_expert_w"][0]], axis=1),
        "b_router": np.concatenate([a["router_group_b"][0], a["router_expert_b"][0]], axis=0),
        "w_gate": a["moe_w_gate"][0],
        "w_up": a["moe_w_up"][0],
        "w_down": a["moe_w_down"][0],
    }
    arrays = {k: np.ascontiguousarray(v) for k, v in arrays.items()}
    nc = bacc.Bacc("TRN2", target_bir_lowering=False, num_devices=1, dynamic_dma_scratch_size=4096)
    args = [nc.dram_tensor(k, v.shape, mybir.dt.from_np(v.dtype), kind="ExternalInput").ap() for k, v in arrays.items()]
    out = nc.dram_tensor("out", (SEQ, D), F32, kind="ExternalOutput").ap()
    hymba_block(nc, *args, out)
    r = run_bass_kernel_spmd(nc, [arrays], core_ids=[0])
    return r.results[0]["out"].reshape(1, SEQ, D)
```

```python
from contextlib import ExitStack

import concourse.bass as bass
from concourse import mybir

P = 128
D = 1024
SEQ = 4096
META = 16
PAD = P - META
TILES = SEQ // P + 1
KT = D // P
LRU = 512
H = 4
CW = 4
PROJ = 3080
NG = 4
EPG = 8
NE = NG * EPG
FE = 256
EPS = 1e-6
LEVELS = range(2, 8)
NBLK = (2 * SEQ + NE * (P - 1)) // P
SURE = 2 * SEQ // P
FEWEST = SURE // 2 - 1
TCAP = SEQ
IDX_FILLS = NE * TCAP // P // 512
WSLOTS = 4
GU = 2 * KT * FE
WD = 2 * D
SLOT = GU + WD
RSTEPS = 20

ALU = mybir.AluOpType
ACT = mybir.ActivationFunctionType
AX = mybir.AxisListType.X
F32 = mybir.dt.float32
BF16 = mybir.dt.bfloat16
I32 = mybir.dt.int32
U32 = mybir.dt.uint32

COL = {"xb": 0, "gb": 512, "q": 1024, "k": 1536, "v": 2048, "z": 2560, "ba": 3072}
GROUPS = ["xb", "q", "k", "v", "gb", "z"]
LOOP = (4, TILES - 2)


def bcast(ap, shape):
    return ap.to_broadcast(shape)


class Step:

    def __init__(self, i):
        self.i = i
        self.F, self.nF, self.pF = self.counts(i + 3, TILES)
        self.P, self.nP, self.pP = self.counts(i + 2, TILES)
        self.G, self.nG, self.pG = self.counts(i + 1, TILES)
        self.O, self.nO, self.pO = self.counts(i - 1, TILES - 1)
        self.R, self.nR, self.pR = self.counts(i - 2, TILES - 1)

    @staticmethod
    def counts(n, most):
        if not isinstance(n, int):
            return True, n, n - 1
        after, before = min(max(n, 0), most), min(max(n - 1, 0), most)
        return after != before, after, before


def steps(eng, body):
    for i in range(-2, LOOP[0]):
        body(Step(i))
    with eng.Fori(LOOP[0], LOOP[1]) as i:
        body(Step(i))
    for i in range(LOOP[1], TILES + 2):
        body(Step(i))


def need(eng, sem, value):
    if not (isinstance(value, int) and value <= 0):
        eng.wait_ge(sem, value)


def hymba_block(nc, xm, w_in, w_out, conv_w, lru_cols, w_r, w_i, mix_g, ffn_g, final_g, dn_g, dn_a,
                dn_dt, w_router, b_router, w_gate, w_up, w_down, out):
    with ExitStack() as ctx:
        def sb(name, shape, dt=F32):
            return ctx.enter_context(nc.sbuf_tensor(name, shape, dt))

        sems = {}

        def sem(name):
            if name not in sems:
                sems[name] = nc.alloc_semaphore(name=name)
            return sems[name]

        def settle(eng):
            eng.sem_inc(sem("settled"), 1)

        def retire(keep):
            nc.all_engine_barrier()
            done = {n: s for n, s in sems.items() if n not in keep}
            nums = sorted(s.num for s in done.values())
            runs = [[nums[0], nums[0] + 1]]
            for n in nums[1:]:
                if n == runs[-1][1]:
                    runs[-1][1] += 1
                else:
                    runs.append([n, n + 1])
            for a, b in runs:
                nc.sync.sem_clear(range(a, b))
            nc.all_engine_barrier()
            for n, s in done.items():
                nc.release_semaphore(s)
                del sems[n]

        h_rows = nc.dram_tensor("h_rows", [SEQ, D], F32, kind="Internal").ap()
        u_rows = nc.dram_tensor("u_rows", [SEQ, D], F32, kind="Internal").ap()
        y_rows = nc.dram_tensor("y_rows", [(NBLK + 1) * P, D], F32, kind="Internal").ap()
        idx_tab = nc.dram_tensor("idx_tab", [NE * TCAP, 1], I32, kind="Internal").ap()
        blk_tab = nc.dram_tensor("blk_tab", [P, 3], I32, kind="Internal").ap()

        W = sb("W", [P, KT * PROJ + KT * D])
        wi = W[:, 0:KT * PROJ].rearrange("p (k n) -> p k n", k=KT)
        wo = W[:, KT * PROJ:KT * PROJ + KT * D].rearrange("p (k n) -> p k n", k=KT)
        wr_bd = sb("wr_bd", [P, 4, P])
        wi_bd = sb("wi_bd", [P, 4, P])
        w_rt = sb("w_rt", [P, KT, NG + NE])

        ident = sb("ident", [P, P])
        ones = sb("ones", [P, P])
        tri = sb("tri", [P, P])
        tri_s = sb("tri_s", [P, P])
        lvl = sb("lvl", [P, 7, P])
        cvw = sb("cvw", [P, 16, CW])
        lcol = sb("lcol", [P, 5, 4])
        cl = sb("cl", [P, 4])
        cl_t = sb("cl_t", [P, 4])
        mg = sb("mg", [P, KT])
        fg = sb("fg", [P, KT])
        dng = sb("dng", [P, P])
        nexp_a = sb("nexp_a", [P, H])
        dt_b = sb("dt_b", [P, H])
        rb = sb("rb", [P, NG + NE])
        eps = sb("eps", [P, 1])
        tiny = sb("tiny", [P, 1])
        iota_e = sb("iota_e", [P, NE])
        iota_p = sb("iota_p", [P, 1])
        io_i = sb("io_i", [P, NE], I32)
        ip_i = sb("ip_i", [P, 1], I32)

        x_in = sb("x_in", [P, D])
        uT = sb("uT", [P, KT, P])
        junk = sb("junk", [P, D], BF16)
        xst = sb("xst", [P, 3])
        ext = [sb(f"ext_{g}", [P, 4, P + 3]) for g in ("xb", "q", "k", "v")]
        xc, qs, ks, vs = (sb(n, [P, 4, P]) for n in ("xc", "qs", "ks", "vs"))
        hT = sb("hT", [P, KT, P])
        la, th = hT[:, 0:4, :], hT[:, 4:8, :]
        gx = sb("gx", [P, 4, P])
        gg = sb("gg", [P, 4, P])
        zg = sb("zg", [P, 4, P])
        sgb = sb("sgb", [P, H])
        al = sb("al", [P, H])
        rnq = sb("rnq", [P, 4, P])
        rnk = sb("rnk", [P, 4, P])
        qh = sb("qh", [P, 4, P])
        kh = sb("kh", [P, 4, P])
        vn, ot, Y = rnq, rnk, qh
        dec = sb("dec", [P, 4, P])
        T = dec
        Mt = sb("Mt", [P, 4, P])
        ML = [sb(f"ML{n}", [P, 4, P]) for n in range(2)]
        X = sb("X", [P, 4, P])
        kd = sb("kd", [P, 4, P])
        vt = sb("vt", [P, 4, P])
        qkT = sb("qkT", [P, 4, P])
        yt = sb("yt", [P, 4, P])
        St = sb("St", [P, 4, P])
        beta = sb("beta", [P, H])
        g4 = sb("g4", [P, H])
        ga = sb("ga", [P, H])
        gl8 = sb("gl8", [P, 8])
        eg8 = sb("eg8", [P, 8])
        neg = sb("neg", [P, H])
        ekd = sb("ekd", [P, H])
        oss = sb("oss", [P, H])
        ors = sb("ors", [P, H])
        aa = sb("aa", [P, 4, P])
        hh = sb("hh", [P, 4, P])
        hlast = sb("hlast", [P, 4])
        lrs = sb("lrs", [P, P])
        yl = sb("yl", [P, 4, P])
        ydT = yt
        ht = sb("ht", [P, D])
        hst = sb("hst", [P, 3])
        lg = sb("lg", [P, NG + NE])
        rg8 = sb("rg8", [P, 8])
        m8 = sb("m8", [P, 8])
        i8 = sb("i8", [P, 8], U32)
        v8 = sb("v8", [P, 8])
        j8 = sb("j8", [P, 8], U32)
        rsm = sb("rsm", [P, 16])
        eg = sb("eg", [P, NG])
        ohg = sb("ohg", [P, NG])
        elg = sb("elg", [P, EPG, NG])
        el8 = sb("el8", [P, EPG])
        oh = sb("oh", [P, 2, NE])
        ohs = sb("ohs", [P, NE])
        pre = sb("pre", [P, NE])
        jr = sb("jr", [P, NE])
        cnt = sb("cnt", [P, NE])
        rt6 = sb("rt6", [P, 6])
        posf = sb("posf", [P, 2])
        posi = sb("posi", [P, 2], I32)
        tokf = sb("tokf", [P, 1])
        toki = sb("toki", [P, 1], I32)
        saved = sb("saved", [P, SEQ // P, 6])

        pj = [ctx.enter_context(nc.psum_tensor(f"pj{n}", [P, 4, P], F32)) for n in range(2)]
        bA = ctx.enter_context(nc.psum_tensor("bA", [P, 4, P], F32))
        bB = ctx.enter_context(nc.psum_tensor("bB", [P, 4, P], F32))
        bC = ctx.enter_context(nc.psum_tensor("bC", [P, 4, P], F32))
        bT = ctx.enter_context(nc.psum_tensor("bT", [P, 4, P], F32))
        bO = ctx.enter_context(nc.psum_tensor("bO", [P, 8, P], F32))
        bTf = bT[:].rearrange("p a b -> p (a b)")
        bOf = bO[:].rearrange("p a b -> p (a b)")

        with nc.Block() as block:
            @block.sync
            def _(sp):
                sp.dma_start(x_in[:], xm[0:P, :]).then_inc(sem("x_in"), 16)
                sp.wait_ge(sem("small_in"), 16 * 8)
                sp.wait_ge(sem("bd_in"), 64)
                for g in GROUPS:
                    c, wide = COL[g], 512 if g != "z" else PROJ - COL["z"]
                    sp.dma_start(wi[:, :, c:c + wide], w_in.rearrange("(p k) n -> p k n", k=KT)[:, :, c:c + wide]
                                 ).then_inc(sem(f"w_{g}_in"), 16)
                sp.dma_start(wo, w_out.rearrange("(k p) n -> p k n", p=P)).then_inc(sem("w_out_in"), 16)
                sp.dma_start(w_rt[:], w_router.rearrange("(p k) n -> p k n", k=KT)).then_inc(sem("w_rt_in"), 16)

            @block.scalar
            def _(act):
                n = 0
                for dst, src in ((cvw[:], conv_w), (lcol[:], lru_cols), (mg[:], mix_g), (fg[:], ffn_g),
                                 (dng[:], dn_g.partition_broadcast(P)), (nexp_a[:], dn_a.partition_broadcast(P)),
                                 (dt_b[:], dn_dt.partition_broadcast(P)), (rb[:], b_router.partition_broadcast(P))):
                    act.dma_start(dst, src).then_inc(sem("small_in"), 16)
                    n += 16
                act.wait_ge(sem("blocks_zero"), 1)
                for dst, src in ((wr_bd, w_r), (wi_bd, w_i)):
                    pair = src.rearrange("(j b) c d -> b c j d", b=2)
                    for b in range(2):
                        act.dma_start(dst[64 * b:64 * b + 64, :, 64 * b:64 * b + 64], pair[b]).then_inc(sem("bd_in"), 16)
                act.wait_ge(sem("small_in"), n)
                act.wait_ge(sem("bd_in"), 64)
                nc.scalar.activation(nexp_a[:], nexp_a[:], ACT.Exp).then_inc(sem("exp_a"), 1)
                nc.scalar.activation(cl[:], lcol[:, 3, :], ACT.Abs).then_inc(sem("cl_s"), 1)
                act.wait_ge(sem("cl_s"), 1)
                nc.scalar.activation(cl[:], cl[:], ACT.Exp, scale=-1.0).then_inc(sem("cl_s"), 1)
                act.wait_ge(sem("cl_s"), 2)
                nc.scalar.activation(cl[:], cl[:], ACT.Ln, bias=1.0).then_inc(sem("cl_s"), 1)

            @block.vector
            def _(dve):
                for t in ext:
                    nc.vector.memset(t[:], 0.0)
                nc.vector.memset(St[:], 0.0)
                nc.vector.memset(hlast[:], 0.0)
                nc.vector.memset(cnt[:], 0.0)
                nc.vector.memset(rg8[:], -3.0e38)
                nc.vector.memset(eps[:], EPS)
                nc.vector.memset(tiny[:], 1e-19).then_inc(sem("dve_const"), 1)
                dve.wait_ge(sem("exp_a"), 1)
                nc.vector.tensor_scalar(nexp_a[:], nexp_a[:], -1.0, None, ALU.mult).then_inc(sem("nexp"), 1)
                dve.wait_ge(sem("cl_s"), 3)
                nc.vector.tensor_scalar(cl_t[:], lcol[:, 3, :], -1.0, 0.0, ALU.mult, ALU.max).then_inc(sem("cl_d"), 1)
                dve.wait_ge(sem("cl_d"), 1)
                nc.vector.tensor_tensor(cl[:], cl[:], cl_t[:], ALU.add).then_inc(sem("cl_d"), 1)
                dve.wait_ge(sem("cl_d"), 2)
                nc.vector.tensor_scalar(cl[:], cl[:], -8.0, None, ALU.mult).then_inc(sem("cl_d"), 1)
                dve.wait_ge(sem("iota_i"), 2)
                nc.vector.tensor_copy(iota_e[:], io_i[:])
                nc.vector.tensor_copy(iota_p[:], ip_i[:])
                nc.vector.tensor_copy(tokf[:], ip_i[:]).then_inc(sem("iota_f"), 1)
                dve.wait_ge(sem("iota_f"), 1)

            @block.gpsimd
            def _(pool):
                nc.gpsimd.memset(wr_bd[:], 0.0)
                nc.gpsimd.memset(wi_bd[:], 0.0).then_inc(sem("blocks_zero"), 1)
                nc.gpsimd.iota(io_i[:], pattern=[[1, NE]], base=0, channel_multiplier=0).then_inc(sem("iota_i"), 1)
                nc.gpsimd.iota(ip_i[:], pattern=[[0, 1]], base=0, channel_multiplier=1).then_inc(sem("iota_i"), 1)
                nc.gpsimd.memset(ht[:, 0:512].bitcast(I32), 0).then_inc(sem("zero_i"), 1)
                nc.gpsimd.memset(ones[:], 1.0).then_inc(sem("p_const"), 1)
                pool.wait_ge(sem("zero_i"), 1)
                zt = ht[:, 0:512].bitcast(I32)
                for n in range(IDX_FILLS):
                    pool.dma_start(idx_tab.rearrange("(p n) o -> p (n o)", p=P)[:, 512 * n:512 * n + 512],
                                   zt).then_inc(sem("idx_zeroed"), 16)
                pool.wait_ge(sem("p_const"), 1)
                nc.gpsimd.affine_select(out=ident[:], in_=ones[:], compare_op=ALU.is_equal, fill=0.0, base=0,
                                        pattern=[[1, P]], channel_multiplier=-1).then_inc(sem("p_const"), 1)
                nc.gpsimd.affine_select(out=tri[:], in_=ones[:], compare_op=ALU.is_ge, fill=0.0, base=0,
                                        pattern=[[1, P]], channel_multiplier=-1).then_inc(sem("p_const"), 1)
                nc.gpsimd.affine_select(out=tri_s[:], in_=ones[:], compare_op=ALU.is_gt, fill=0.0, base=0,
                                        pattern=[[1, P]], channel_multiplier=-1).then_inc(sem("p_const"), 1)
                pool.wait_ge(sem("p_const"), 4)
                done = 4
                for l in range(1, 8):
                    b = 1 << l
                    m = lvl[:, l - 1, :]
                    mv = m.rearrange("p (n c) -> p n c", c=b)
                    src = tri_s[:].rearrange("p (n c) -> p n c", c=b)
                    nc.gpsimd.affine_select(out=mv, in_=src, compare_op=ALU.is_ge, fill=0.0, base=0,
                                            pattern=[[-b, P // b], [0, b]], channel_multiplier=1).then_inc(sem("p_const"), 1)
                    done += 1
                    pool.wait_ge(sem("p_const"), done)
                    nc.gpsimd.affine_select(out=mv, in_=mv, compare_op=ALU.is_ge, fill=0.0, base=b // 2 - 1,
                                            pattern=[[b, P // b], [0, b]], channel_multiplier=-1).then_inc(sem("p_const"), 1)
                    done += 1
                    pool.wait_ge(sem("p_const"), done)
                    nc.gpsimd.affine_select(out=mv, in_=mv, compare_op=ALU.is_ge, fill=0.0, base=-(b // 2),
                                            pattern=[[0, P // b], [1, b]], channel_multiplier=0).then_inc(sem("p_const"), 1)
                    done += 1
                    pool.wait_ge(sem("p_const"), done)

        weights_in = [f"w_{g}_in" for g in GROUPS] + ["w_out_in", "w_rt_in"]
        retire(keep=["idx_zeroed", "x_in"] + weights_in)

        def load_expert(sp, e, slot):
            o = slot * SLOT
            for a, b, src in ((o, o + KT * FE, w_gate[bass.ds(e, 1)].rearrange("o (p k) f -> p (o k f)", k=KT)),
                              (o + KT * FE, o + GU, w_up[bass.ds(e, 1)].rearrange("o (p k) f -> p (o k f)", k=KT)),
                              (o + GU, o + SLOT, w_down[bass.ds(e, 1)].rearrange("o (p j) n -> p (o j n)", j=2))):
                sp.dma_start(W[:, a:b], src).then_inc(sem(f"w_loaded{slot}"), 16)

        def flat(t):
            return t[:].rearrange("p a b -> p (a b)")

        def rows(t):
            return t.unsqueeze(2).to_broadcast([P, 4, P])

        def cols(t):
            return t.unsqueeze(1).to_broadcast([P, 4, P])

        with nc.Block() as block:
            @block.sync
            def _(sp):
                def body(s):
                    if s.F and not (isinstance(s.i, int) and s.nF == 1):
                        need(sp, sem("x_turned"), s.pF)
                        settle(sp)
                        sp.dma_start(x_in[:], xm[bass.ds((s.i + 2) * P, P), :]).then_inc(sem("x_in"), 16)
                    if s.O:
                        need(sp, sem("h_turned"), s.nR)
                        settle(sp)
                        need(sp, sem("u_stored"), 32 * s.pO)
                        settle(sp)
                        if isinstance(s.i, int) and s.nO == 1:
                            sp.wait_ge(sem("idx_zeroed"), 16 * IDX_FILLS)
                        sp.dma_start(ht[:], xm[bass.ds(s.nO * P, P), :]).then_inc(sem("x_res"), 16)
                        if isinstance(s.i, int) and s.i == TILES - 1:
                            sp.wait_ge(sem("ba_full"), TILES)
                            for slot in range(WSLOTS):
                                load_expert(sp, slot, slot)
                        need(sp, sem("h_ready"), s.nO)
                        settle(sp)
                        sp.dma_start(h_rows[bass.ds(s.pO * P, P), :], ht[:]).then_inc(sem("h_stored"), 16)
                        need(sp, sem("u2_ready"), s.nO)
                        settle(sp)
                        sp.dma_start(u_rows[bass.ds(s.pO * P, P), :], ht[:]).then_inc(sem("u_stored"), 16)
                        sp.dma_start(y_rows[bass.ds((s.pO + SURE) * P, P), :], ht[:]).then_inc(sem("u_stored"), 16)
                steps(sp, body)
                sp.wait_ge(sem("h_stored"), 16 * (TILES - 1))
                sp.wait_ge(sem("u_stored"), 32 * (TILES - 1))

            @block.tensor
            def _(pe):
                def project(s, n):
                    if not s.P:
                        return
                    g, j = divmod(n, 4)
                    if n == 0:
                        need(pe, sem("uT_ready"), s.nP)
                    if j == 0:
                        free, v = (("gb_used", s.pP), ("z_used", s.pP), ("xb_evac", s.nP), ("q_evac", s.nP),
                                   ("k_evac", s.nP))[g]
                        need(pe, sem(free), v)
                    if j == 0 and isinstance(s.i, int) and s.nP == 1:
                        pe.wait_ge(sem(f"w_{GROUPS[g]}_in"), 16)
                    c = COL[GROUPS[g]] + j * P
                    for k in range(KT):
                        mm = pe.matmul(pj[g % 2][:, j, :], wi[:, k, c:c + P], uT[:, k, :], start=(k == 0), stop=(k == KT - 1))
                    if j == 3:
                        mm.then_inc(sem(GROUPS[g] + "_full"), 1)

                def project_z(s, n):
                    if not s.P:
                        return
                    if n == 0:
                        need(pe, sem("v_evac"), s.nP)
                    if n == 0 and isinstance(s.i, int) and s.nP == 1:
                        pe.wait_ge(sem("w_z_in"), 16)
                    c = COL["z"]
                    for k in (2 * n, 2 * n + 1):
                        mm = pe.matmul(flat(pj[1]), uT[:, k, :], wi[:, k, c:c + 512], start=(k == 0), stop=(k == KT - 1))
                    if n == 3:
                        mm.then_inc(sem("z_full"), 1)

                def w_out_part(s, n):
                    if not s.O:
                        return
                    half, m = divmod(n, 4)
                    if n == 0:
                        if isinstance(s.i, int) and s.nO == 1:
                            pe.wait_ge(sem("w_out_in"), 16)
                        need(pe, sem("ydT_ready"), s.nO)
                        need(pe, sem("yl_ready"), s.nO + 1)
                        need(pe, sem("hT_ready"), s.nR)
                        need(pe, sem("uT_ready"), s.pF)
                    for j in (2 * m, 2 * m + 1):
                        lhs = yl[:, j, :] if j < 4 else ydT[:, j - 4, :]
                        mm = pe.matmul(bOf[:, 512 * half:512 * half + 512], lhs, wo[:, j, 512 * half:512 * half + 512],
                                       start=(j == 0), stop=(j == 7))
                    if n == 7:
                        mm.then_inc(sem("wo_full"), 1)

                def fill(s, n):
                    if n < 8:
                        project(s, 12 + n)
                    elif n < 12:
                        project_z(s, n - 8)
                    else:
                        w_out_part(s, n - 12)

                def body(s):
                    if s.R:
                        need(pe, sem("u2_ready"), s.nR)
                        need(pe, sem("uT_ready"), s.pF)
                        for k in range(KT):
                            mm = pe.transpose(bO[:, k, :], ht[:, k:D:KT], ident[:])
                        mm.then_inc(sem("h_turned"), 1)
                    project(s, 0)
                    project(s, 1)
                    project(s, 2)
                    if s.G:
                        need(pe, sem("sq_k"), s.nG)
                        need(pe, sem("r_gate"), s.pP)
                        pe.matmul(flat(bB), ones[:], flat(rnk), start=True, stop=True).then_inc(sem("nk_full"), 1)
                        need(pe, sem("sq_q"), s.nG)
                        need(pe, sem("S_new"), s.pG)
                        pe.matmul(flat(bA), ones[:], flat(rnq), start=True, stop=True).then_inc(sem("nq_full"), 1)
                    project(s, 3)
                    if s.G:
                        need(pe, sem("g_ready"), s.nG)
                        need(pe, sem("al_ready"), s.pP)
                        need(pe, sem("sgb_ready"), s.pP)
                        pe.matmul(bTf[:, 0:H], tri[:], g4[:], start=True, stop=True)
                        pe.matmul(bTf[:, H:2 * H], ones[:], g4[:], start=True, stop=True).then_inc(sem("cum_full"), 1)
                        need(pe, sem("gtri_ready"), s.nG)
                        need(pe, sem("i_gate"), s.pP)
                        pe.matmul(flat(bC), ones[:], flat(dec), start=True, stop=True).then_inc(sem("grow_full"), 1)
                    for n in (4, 5, 6):
                        project(s, n)
                    if s.G:
                        need(pe, sem("kh_ready"), s.nG)
                        need(pe, sem("gl8_ready"), s.nG)
                        for h in range(H):
                            mm = pe.transpose(bT[:, h, :], kh[:, h, :], ident[:])
                        mm.then_inc(sem("kt_full"), 1)
                        need(pe, sem("qh_ready"), s.nG)
                        need(pe, sem("nq_used"), s.nG)
                        for h in range(H):
                            mm = pe.matmul(bA[:, h, :], kh[:, h, :], kh[:, h, :], start=True, stop=True)
                        mm.then_inc(sem("kk_full"), 1)
                        need(pe, sem("nk_used"), s.nG)
                        for h in range(H):
                            mm = pe.matmul(bB[:, h, :], kh[:, h, :], qh[:, h, :], start=True, stop=True)
                        mm.then_inc(sem("qk_full"), 1)
                        need(pe, sem("dec_sub"), s.nG)
                        need(pe, sem("v_silu"), s.nG)
                        for h in range(H):
                            mm = pe.transpose(bC[:, h, :], vs[:, h, :], ident[:])
                        mm.then_inc(sem("vt_full"), 1)
                    for n in (7, 8):
                        project(s, n)
                    if s.O:
                        need(pe, sem("yt_ready"), s.nO + 1)
                        need(pe, sem("kd_ready"), s.nG)
                        if not s.G:
                            need(pe, sem("lrs_ln"), s.nG)
                        for h in range(H):
                            mm = pe.transpose(bT[:, h, :], yt[:, h, :], ident[:])
                        mm.then_inc(sem("ydT_full"), 1)
                    for n in (9, 10):
                        project(s, n)
                    if s.G:
                        need(pe, sem("X_first"), s.nG)
                        need(pe, sem("ydT_ready"), s.nO)
                        if not s.O:
                            need(pe, sem("kd_ready"), s.nG)
                        for h in range(H):
                            mm = pe.transpose(bT[:, h, :], X[:, h, :], ident[:])
                        mm.then_inc(sem("T_full"), 1)
                        need(pe, sem("vt_ready"), s.nG)
                        need(pe, sem("S_new"), s.pG)
                        for h in range(H):
                            mm = pe.matmul(bC[:, h, :], kh[:, h, :], St[:, h, :], start=True, stop=True)
                        mm.then_inc(sem("kS_full"), 1)
                        need(pe, sem("M_raw"), s.nG)
                        for h in range(H):
                            mm = pe.matmul(bA[:, h, :], qh[:, h, :], St[:, h, :], start=True, stop=True)
                        mm.then_inc(sem("qS_full"), 1)
                    project(s, 11)
                    if s.R:
                        need(pe, sem("hT_ready"), s.nR)
                        if isinstance(s.i, int) and s.nR == 1:
                            pe.wait_ge(sem("w_rt_in"), 16)
                        if s.G:
                            need(pe, sem("T_new"), 6 * s.pG + 1)
                        else:
                            need(pe, sem("ydT_ready"), s.nO)
                            need(pe, sem("rank_used"), s.pR)
                        for k in range(KT):
                            mm = pe.matmul(bTf[:, 0:NG + NE], hT[:, k, :], w_rt[:, k, :], start=(k == 0), stop=(k == KT - 1))
                        mm.then_inc(sem("rt_full"), 1)
                    for l in LEVELS:
                        n = 3 * (l - 2)
                        if s.G:
                            c = 6 * s.pG + l - 1
                            need(pe, sem("ML_ready"), c)
                            need(pe, sem("T_new"), c)
                            if l == 2:
                                need(pe, sem("o1_ready"), s.nG)
                            for h in range(H):
                                mm = pe.matmul(bA[:, h, :], ML[l % 2][:, h, :], T[:, h, :], start=True, stop=True)
                            mm.then_inc(sem("Y_full"), 1)
                        fill(s, n)
                        if s.G:
                            need(pe, sem("Y_new"), c)
                            need(pe, sem("qkT_ready"), s.nG) if l == 2 else need(pe, sem("X_new"), c - 1)
                            for h in range(H):
                                mm = pe.matmul(bB[:, h, :], Y[:, h, :], X[:, h, :], start=True, stop=True)
                            mm.then_inc(sem("XU_full"), 1)
                        fill(s, n + 1)
                        if l < 7:
                            if s.G:
                                need(pe, sem("X_new"), c)
                                if l == 2:
                                    need(pe, sem("lg_ready"), s.nR)
                                if l == 6:
                                    need(pe, sem("rank_used"), s.nR)
                                for h in range(H):
                                    mm = pe.transpose(bT[:, h, :], X[:, h, :], ident[:])
                                mm.then_inc(sem("T_full"), 1)
                            fill(s, n + 2)
                        if l == 5 and s.R:
                            need(pe, sem("oh_ready"), s.nR)
                            need(pe, sem("lg_ready"), s.nR)
                            if s.G:
                                need(pe, sem("T_new"), 6 * s.pG + 5)
                            pe.matmul(bTf[:, 0:NE], tri_s[:], ohs[:], start=True, stop=True)
                            pe.matmul(bTf[:, NE:2 * NE], ones[:], ohs[:], start=True, stop=True).then_inc(sem("rank_full"), 1)
                    if s.G:
                        need(pe, sem("R_ready"), s.nG)
                        need(pe, sem("X_new"), 6 * s.nG)
                        for h in range(H):
                            mm = pe.matmul(bB[:, h, :], X[:, h, :], vt[:, h, :], start=True, stop=True)
                        mm.then_inc(sem("vn_full"), 1)
                    fill(s, 17)
                    if s.G:
                        need(pe, sem("vn_ready"), s.nG)
                        for h in range(H):
                            mm = pe.matmul(bC[:, h, :], qkT[:, h, :], vn[:, h, :], start=True, stop=True)
                        mm.then_inc(sem("intra_full"), 1)
                        need(pe, sem("kd_ready"), s.nG)
                        need(pe, sem("Y_new"), 6 * s.nG)
                        for h in range(H):
                            mm = pe.matmul(bA[:, h, :], kd[:, h, :], vn[:, h, :], start=True, stop=True)
                        mm.then_inc(sem("Su_full"), 1)
                    fill(s, 18)
                    fill(s, 19)
                    if s.G:
                        need(pe, sem("y_sq"), s.nG)
                        need(pe, sem("T_new"), 6 * s.nG)
                        need(pe, sem("rank_used"), s.nR)
                        for j in range(4):
                            mm = pe.matmul(bT[:, 0, :], ones[:], aa[:, j, :], start=(j == 0), stop=(j == 3))
                        mm.then_inc(sem("lnorm_full"), 1)
                    if s.P:
                        need(pe, sem("conv"), 16 * s.pP + 4)
                        need(pe, sem("vn_ready"), s.nG)
                        for j in range(4):
                            mm = pe.matmul(bB[:, j, :], wr_bd[:, j, :], xc[:, j, :], start=True, stop=True)
                        mm.then_inc(sem("gr_full"), 1)
                        need(pe, sem("o_ready"), s.nG)
                        for j in range(4):
                            mm = pe.matmul(bC[:, j, :], wi_bd[:, j, :], xc[:, j, :], start=True, stop=True)
                        mm.then_inc(sem("gi_full"), 1)
                        need(pe, sem("lrs_ln"), s.nG)
                        c = COL["ba"]
                        for k in range(KT):
                            mm = pe.matmul(bTf[:, 0:2 * H], uT[:, k, :], wi[:, k, c:c + 2 * H], start=(k == 0), stop=(k == KT - 1))
                        mm.then_inc(sem("ba_full"), 1)
                    if s.F:
                        need(pe, sem("u_ready"), s.nF)
                        need(pe, sem("h_ready"), s.nO)
                        for k in range(KT):
                            mm = pe.transpose(bO[:, k, :], x_in[:, k:D:KT], ident[:])
                        mm.then_inc(sem("x_turned"), 1)
                steps(pe, body)

            @block.scalar
            def _(act):
                def evac(s, g, name, n):
                    if s.P:
                        need(act, sem(name + "_full"), s.nP)
                        need(act, sem("halo"), 4 * s.pP - 3 + n)
                        nc.scalar.activation(ext[g][:, :, 3:3 + P], pj[n % 2][:], ACT.Copy).then_inc(sem(name + "_evac"), 1)

                def rsqrt(src, dst, scale, bias, ln_sem, out_sem):
                    nc.scalar.activation(dst, src, ACT.Ln, scale=scale, bias=bias).then_inc(sem(ln_sem[0]), 1)
                    need(act, sem(ln_sem[0]), ln_sem[1])
                    nc.scalar.activation(dst, dst, ACT.Exp, scale=-0.5).then_inc(sem(out_sem), 1)

                def body(s):
                    nc.scalar.preload_act_table_set("natural_log_exp_and_others")
                    if s.G:
                        need(act, sem("k_silu"), s.nG)
                        need(act, sem("yt_ready"), s.pG)
                        nc.scalar.activation(rnk[:], ks[:], ACT.Square).then_inc(sem("sq_k"), 1)
                        need(act, sem("q_silu"), s.nG)
                        need(act, sem("S_new"), s.pG)
                        need(act, sem("intra_full"), s.pG)
                        nc.scalar.activation(rnq[:], qs[:], ACT.Square).then_inc(sem("sq_q"), 1)
                        need(act, sem("al_ready"), s.nG)
                        need(act, sem("g_ready"), s.pG)
                        nc.scalar.activation(ga[:], al[:], ACT.Abs).then_inc(sem("g_ln"), 1)
                        need(act, sem("g_ln"), 3 * s.pG + 1)
                        nc.scalar.activation(ga[:], ga[:], ACT.Exp, scale=-1.0).then_inc(sem("g_ln"), 1)
                        need(act, sem("g_ln"), 3 * s.pG + 2)
                        nc.scalar.activation(ga[:], ga[:], ACT.Ln, bias=1.0).then_inc(sem("g_ln"), 1)
                        need(act, sem("nk_full"), s.nG)
                        rsqrt(bB[:], rnk[:], 1.0, eps[:], ("nk_used", s.nG), "rk_ready")
                        need(act, sem("nq_full"), s.nG)
                        rsqrt(bA[:], rnq[:], 1.0, eps[:], ("nq_used", s.nG), "rq_ready")
                        need(act, sem("la_ready"), s.nG)
                        need(act, sem("lnorm_full"), s.pG)
                        nc.scalar.activation(aa[:], la, ACT.Exp).then_inc(sem("a_exp"), 1)
                        need(act, sem("a_exp"), s.nG)
                        need(act, sem("y_sq"), s.pG)
                        nc.scalar.activation(hh[:], aa[:], ACT.Square).then_inc(sem("a_sq"), 1)
                        need(act, sem("cum_full"), s.nG)
                        need(act, sem("S_new"), s.pG)
                        nc.scalar.activation(gl8[:], bTf[:, 0:8], ACT.Copy).then_inc(sem("gl8_ready"), 1)
                        need(act, sem("gl8_ready"), s.nG)
                        nc.scalar.activation(eg8[:], gl8[:], ACT.Exp).then_inc(sem("eg8_ready"), 1)
                        need(act, sem("ekd_raw"), s.nG)
                        nc.scalar.activation(ekd[:], ekd[:], ACT.Exp).then_inc(sem("ekd_ready"), 1)
                        need(act, sem("dec_min"), s.nG)
                        nc.scalar.activation(dec[:], dec[:], ACT.Exp).then_inc(sem("dec_exp"), 1)
                    evac(s, 0, "xb", 0)
                    if s.G:
                        need(act, sem("w_ready"), s.nG)
                        nc.scalar.activation(hh[:], hh[:], ACT.Ln, bias=tiny[:]).then_inc(sem("w_ln"), 1)
                        need(act, sem("w_ln"), s.nG)
                        nc.scalar.activation(hh[:], hh[:], ACT.Exp, scale=0.5).then_inc(sem("ib_ready"), 1)
                        need(act, sem("vt_full"), s.nG)
                        need(act, sem("vn_full"), s.pG)
                        nc.scalar.activation(vt[:], bC[:], ACT.Copy).then_inc(sem("vt_ready"), 1)
                    evac(s, 1, "q", 1)
                    if s.O:
                        need(act, sem("ydT_full"), s.nO)
                        need(act, sem("wo_full"), s.pO)
                        nc.scalar.activation(ydT[:], bT[:], ACT.Copy).then_inc(sem("ydT_ready"), 1)
                    if s.F:
                        need(act, sem("x_in"), 16 * s.nF)
                        need(act, sem("u_ready"), s.pF)
                        nc.scalar.activation(junk[:], x_in[:], ACT.Square, accum_out=xst[:, 0:1]).then_inc(sem("x_ss"), 1)
                        need(act, sem("x_ss"), s.nF)
                        rsqrt(xst[:, 0:1], xst[:, 1:2], 1.0 / D, eps[:], ("x_ln", s.nF), "x_norm")
                    if s.G:
                        need(act, sem("T_full"), 6 * s.pG + 1)
                        need(act, sem("M_raw"), s.nG)
                        need(act, sem("qkT_ready"), s.nG)
                        nc.scalar.activation(T[:], bT[:], ACT.Copy).then_inc(sem("T_new"), 1)
                    evac(s, 2, "k", 2)
                    for l in LEVELS:
                        if s.G:
                            c = 6 * s.pG + l - 1
                            if l == 2:
                                need(act, sem("qS_full"), s.nG)
                            need(act, sem("Y_full"), c)
                            nc.scalar.activation(Y[:], bA[:], ACT.Copy).then_inc(sem("Y_new"), 1)
                            if l < 7:
                                need(act, sem("T_full"), c + 1)
                                nc.scalar.activation(T[:], bT[:], ACT.Copy).then_inc(sem("T_new"), 1)
                        if l == 3:
                            evac(s, 3, "v", 3)
                        if l == 4 and s.R:
                            need(act, sem("top_ready"), s.nR)
                            nc.scalar.activation(eg[:], rg8[:, 0:NG], ACT.Exp, bias=rsm[:, 0:1],
                                                 accum_out=rsm[:, 2:3]).then_inc(sem("exp_ready"), 1)
                            nc.scalar.activation(rsm[:, 3:4], rsm[:, 1:2], ACT.Exp).then_inc(sem("exp_ready"), 1)
                        if l == 6 and s.P:
                            need(act, sem("gb_full"), s.nP)
                            need(act, sem("y_lru"), s.nG)
                            nc.scalar.activation(gg[:], pj[0][:], ACT.Square).then_inc(sem("gb_sq"), 1)
                        if l == 4 and s.G:
                            need(act, sem("y_lru"), s.nG)
                            nc.scalar.activation(aa[:], hh[:], ACT.Square).then_inc(sem("y_sq"), 1)
                    if s.G:
                        need(act, sem("lnorm_full"), s.nG)
                        need(act, sem("yl_ready"), s.pG)
                        rsqrt(bT[:, 0, :], lrs[:], 1.0 / LRU, eps[:], ("lrs_ln", s.nG), "lrs_ready")
                        need(act, sem("o_ready"), s.nG)
                        need(act, sem("yt_ready"), s.pG)
                        for h in range(H):
                            a = nc.scalar.activation(junk[:, h * P:h * P + P], ot[:, h, :], ACT.Square, accum_out=oss[:, h:h + 1])
                        a.then_inc(sem("o_ss"), 1)
                        need(act, sem("o_ss"), s.nG)
                        rsqrt(oss[:], ors[:], 1.0 / P, eps[:], ("o_ln", s.nG), "o_norm")
                    if s.O:
                        need(act, sem("h_ready"), s.nO)
                        need(act, sem("u2_ready"), s.pO)
                        nc.scalar.activation(junk[:], ht[:], ACT.Square, accum_out=hst[:, 0:1]).then_inc(sem("h_ss"), 1)
                        need(act, sem("h_ss"), s.nO)
                        rsqrt(hst[:, 0:1], hst[:, 1:2], 1.0 / D, eps[:], ("h_ln", s.nO), "h_norm")
                    if s.P:
                        need(act, sem("gelu_arg"), 2 * s.nP)
                        nc.scalar.activation(gg[:], gg[:], ACT.Sigmoid, scale=2 * 0.7978845608028654).then_inc(sem("gelu_sig"), 1)
                        need(act, sem("z_full"), s.nP)
                        need(act, sem("yt_ready"), s.nG)
                        nc.scalar.activation(zg[:], pj[1][:], ACT.Sigmoid).then_inc(sem("z_sig"), 1)
                        need(act, sem("gr_full"), s.nP)
                        need(act, sem("a_exp"), s.nG)
                        need(act, sem("rt_full"), s.nR)
                        for j in range(4):
                            a = nc.scalar.activation(la[:, j, :], bB[:, j, :], ACT.Sigmoid, bias=lcol[:, 1, j:j + 1])
                        a.then_inc(sem("r_gate"), 1)
                        need(act, sem("gi_full"), s.nP)
                        need(act, sem("h_scan"), s.nG)
                        for j in range(4):
                            a = nc.scalar.activation(gx[:, j, :], bC[:, j, :], ACT.Sigmoid, bias=lcol[:, 2, j:j + 1])
                        a.then_inc(sem("i_gate"), 1)
                        need(act, sem("ba_full"), s.nP)
                        need(act, sem("beta_ready"), s.nG)
                        nc.scalar.activation(sgb[:], bTf[:, 0:H], ACT.Sigmoid).then_inc(sem("sgb_ready"), 1)
                        need(act, sem("conv"), 16 * s.nP)
                        need(act, sem("Y_full"), 6 * s.nG)
                        for n, (src, tmp) in enumerate(((ks, ML[0]), (qs, ML[1]), (vs, Mt))):
                            nc.scalar.activation(tmp[:], src[:], ACT.Sigmoid).then_inc(sem("qkv_sig"), 1)
                        need(act, sem("la_ready"), s.nP)
                        need(act, sem("w_ready"), s.nG)
                        nc.scalar.activation(th, la, ACT.Tanh, scale=-1.0).then_inc(sem("th_ready"), 1)
                steps(act, body)

            @block.vector
            def _(dve):
                def conv(s, g, dst):
                    if not s.P:
                        return
                    need(dve, sem(("xb", "q", "k", "v")[g] + "_evac"), s.nP)
                    for tap in range(CW):
                        for j in range(4):
                            w = cvw[:, 4 * g + j, tap:tap + 1]
                            src = ext[g][:, j, tap:tap + P]
                            if tap:
                                a = nc.vector.scalar_tensor_tensor(out=dst[:, j, :], in0=src, scalar=w, in1=dst[:, j, :],
                                                                   op0=ALU.mult, op1=ALU.add)
                            elif g == 0:
                                a = nc.vector.tensor_scalar(dst[:, j, :], src, w, lcol[:, 0, j:j + 1], ALU.mult, ALU.add)
                            else:
                                a = nc.vector.tensor_scalar(dst[:, j, :], src, w, None, ALU.mult)
                        a.then_inc(sem("conv"), 1)
                        dve.wait_ge(sem("conv"), 16 * s.pP + 4 * g + tap + 1)
                    nc.vector.tensor_copy(ext[g][:, :, 0:3], ext[g][:, :, P:P + 3]).then_inc(sem("halo"), 1)

                def link(s, ins, k):
                    ins.then_inc(sem("rt_step"), 1)
                    dve.wait_ge(sem("rt_step"), RSTEPS * s.pR + k)

                def body(s):
                    if s.G:
                        need(dve, sem("g_ln"), 3 * s.nG)
                        need(dve, sem("S_new"), s.pG)
                        need(dve, sem("grow_full"), s.pG)
                        nc.vector.scalar_tensor_tensor(out=g4[:], in0=al[:], scalar=0.0, in1=ga[:], op0=ALU.max,
                                                       op1=ALU.add).then_inc(sem("g_sp"), 1)
                        need(dve, sem("sgb_ready"), s.nG)
                        nc.vector.tensor_copy(beta[:], sgb[:]).then_inc(sem("beta_ready"), 1)
                        need(dve, sem("g_sp"), s.nG)
                        nc.vector.tensor_tensor(g4[:], g4[:], nexp_a[:], ALU.mult).then_inc(sem("g_ready"), 1)
                        need(dve, sem("rk_ready"), s.nG)
                        need(dve, sem("kS_full"), s.pG)
                        nc.vector.tensor_tensor(kh[:], ks[:], rnk[:], ALU.mult).then_inc(sem("kh_ready"), 1)
                        need(dve, sem("rq_ready"), s.nG)
                        need(dve, sem("XU_full"), 6 * s.pG)
                        nc.vector.scalar_tensor_tensor(out=qh[:], in0=qs[:], scalar=P ** -0.5, in1=rnq[:], op0=ALU.mult,
                                                       op1=ALU.mult).then_inc(sem("qh_ready"), 1)
                    if s.G:
                        need(dve, sem("gl8_ready"), s.nG)
                        need(dve, sem("kd_ready"), s.pG)
                        nc.vector.tensor_tensor(ekd[:], gl8[:, 4:8], gl8[:, 0:4], ALU.subtract).then_inc(sem("ekd_raw"), 1)
                        need(dve, sem("eg8_ready"), s.nG)
                        nc.vector.tensor_scalar(neg[:], eg8[:, 0:4], -1.0, None, ALU.mult).then_inc(sem("neg_ready"), 1)
                        need(dve, sem("grow_full"), s.nG)
                        nc.vector.tensor_tensor(dec[:], bC[:], rows(gl8[:, 0:4]), ALU.subtract).then_inc(sem("dec_sub"), 1)
                        need(dve, sem("dec_sub"), s.nG)
                        nc.vector.tensor_scalar(dec[:], dec[:], 0.0, None, ALU.min).then_inc(sem("dec_min"), 1)
                        need(dve, sem("a_sq"), s.nG)
                        need(dve, sem("th_ready"), s.nG)
                        nc.vector.scalar_tensor_tensor(out=hh[:], in0=hh[:], scalar=1.0, in1=th, op0=ALU.add,
                                                       op1=ALU.mult).then_inc(sem("w_ready"), 1)
                    if s.R:
                        need(dve, sem("h_turned"), s.nR)
                        need(dve, sem("rt_full"), s.pR)
                        need(dve, sem("a_exp"), s.nG)
                        need(dve, sem("w_ready"), s.nG)
                        for half in range(2):
                            k = 4 * half
                            a = nc.vector.tensor_tensor(hT[:, k:k + 4, :], bO[:, k:k + 4, :], rows(fg[:, k:k + 4]), ALU.mult)
                        a.then_inc(sem("hT_ready"), 1)
                    if s.P:
                        need(dve, sem("gi_full"), s.pP)
                        need(dve, sem("gx_ready"), s.pP)
                    conv(s, 0, xc)
                    if s.G:
                        need(dve, sem("kt_full"), s.nG)
                        need(dve, sem("ekd_ready"), s.nG)
                        need(dve, sem("Su_full"), s.pG)
                        nc.vector.tensor_tensor(kd[:], bT[:], rows(ekd[:]), ALU.mult).then_inc(sem("kd_ready"), 1)
                        need(dve, sem("kk_full"), s.nG)
                        need(dve, sem("dec_ready"), s.nG)
                        need(dve, sem("ML_ready"), 6 * s.pG)
                        nc.vector.tensor_tensor(Mt[:], bA[:], dec[:], ALU.mult).then_inc(sem("M_raw"), 1)
                        need(dve, sem("qk_full"), s.nG)
                        need(dve, sem("intra_full"), s.pG)
                        nc.vector.tensor_tensor(qkT[:], bB[:], dec[:], ALU.mult).then_inc(sem("qkT_ready"), 1)
                    if s.F:
                        need(dve, sem("x_norm"), s.nF)
                        nc.vector.tensor_scalar(x_in[:], x_in[:], xst[:, 1:2], None, ALU.mult).then_inc(sem("u_ready"), 1)
                    if s.G:
                        need(dve, sem("X_tmp"), s.nG)
                        nc.vector.tensor_tensor(X[:], cols(ident[:]), X[:], ALU.subtract).then_inc(sem("X_first"), 1)
                    conv(s, 1, qs)
                    if s.G:
                        need(dve, sem("kS_full"), s.nG)
                        need(dve, sem("neg_ready"), s.nG)
                        for h in range(H):
                            a = nc.vector.scalar_tensor_tensor(out=vt[:, h, :], in0=bC[:, h, :], scalar=neg[:, h:h + 1],
                                                               in1=vt[:, h, :], op0=ALU.mult, op1=ALU.add)
                        a.then_inc(sem("R_ready"), 1)
                        need(dve, sem("qS_full"), s.nG)
                        nc.vector.tensor_tensor(ot[:], bA[:], rows(eg8[:, 0:4]), ALU.mult).then_inc(sem("o1_ready"), 1)
                        need(dve, sem("b_ready"), s.nG)
                        need(dve, sem("hl_saved"), s.pG)
                        for j in range(4):
                            a = nc.vector.tensor_tensor_scan(out=hh[:, j, :], data0=aa[:, j, :], data1=gx[:, j, :],
                                                             initial=hlast[:, j:j + 1], op0=ALU.mult, op1=ALU.add)
                        a.then_inc(sem("h_scan"), 1)
                        need(dve, sem("h_scan"), s.nG)
                        nc.vector.tensor_copy(hlast[:].unsqueeze(2), hh[:, :, P - 1:P]).then_inc(sem("hl_saved"), 1)
                    if s.R:
                        need(dve, sem("rt_full"), s.nR)
                        nc.vector.tensor_tensor(lg[:], bTf[:, 0:NG + NE], rb[:], ALU.add).then_inc(sem("lg_ready"), 1)
                    for l in LEVELS:
                        if s.G:
                            c = 6 * s.pG + l - 1
                            need(dve, sem("XU_full"), c)
                            need(dve, sem("T_full"), c)
                            nc.vector.tensor_tensor(X[:], X[:], bB[:], ALU.subtract).then_inc(sem("X_new"), 1)
                        if l == 2:
                            conv(s, 2, ks)
                        if l == 3 and s.R:
                            need(dve, sem("lg_ready"), s.nR)
                            link(s, nc.vector.tensor_copy(rg8[:, 0:NG], lg[:, 0:NG]), 1)
                            settle(dve)
                            link(s, nc.vector.max(m8[:], rg8[:]), 2)
                            settle(dve)
                            link(s, nc.vector.max_index(i8[:], m8[:], rg8[:]), 3)
                            nc.vector.tensor_scalar(rsm[:, 0:1], m8[:, 0:1], -1.0, None, ALU.mult)
                            link(s, nc.vector.tensor_copy(rsm[:, 4:5], i8[:, 0:1]), 4)
                            nc.vector.tensor_scalar(rsm[:, 5:6], rsm[:, 4:5], float(EPG), None, ALU.mult)
                            link(s, nc.vector.tensor_scalar(ohg[:], iota_e[:, 0:NG], rsm[:, 4:5], None, ALU.is_equal), 5)
                            link(s, nc.vector.tensor_tensor(elg[:], lg[:, NG:].rearrange("p (g e) -> p e g", g=NG),
                                                            ohg[:].unsqueeze(1).to_broadcast([P, EPG, NG]), ALU.mult), 6)
                            link(s, nc.vector.tensor_reduce(el8[:], elg[:], AX, ALU.add), 7)
                            settle(dve)
                            link(s, nc.vector.max(v8[:], el8[:]), 8)
                            nc.vector.tensor_tensor(rsm[:, 1:2], v8[:, 1:2], v8[:, 0:1], ALU.subtract).then_inc(sem("top_ready"), 1)
                            settle(dve)
                            link(s, nc.vector.max_index(j8[:], v8[:], el8[:]), 9)
                            link(s, nc.vector.tensor_copy(rsm[:, 6:8], j8[:, 0:2]), 10)
                            need(dve, sem("saved_ready"), s.pR)
                            link(s, nc.vector.tensor_scalar(rt6[:, 0:2], rsm[:, 6:8], rsm[:, 5:6], None, ALU.add), 11)
                            need(dve, sem("rank_full"), s.pR)
                            for a in range(2):
                                ins = nc.vector.tensor_scalar(oh[:, a, :], iota_e[:], rt6[:, a:a + 1], None, ALU.is_equal)
                            link(s, ins, 12)
                            nc.vector.tensor_tensor(ohs[:], oh[:, 0, :], oh[:, 1, :], ALU.add).then_inc(sem("oh_ready"), 1)
                        if l == 5:
                            conv(s, 3, vs)
                            if s.R:
                                need(dve, sem("rank_full"), s.nR)
                                link(s, nc.vector.tensor_tensor(pre[:], bTf[:, 0:NE], cnt[:], ALU.add), 13)
                                nc.vector.tensor_tensor(cnt[:], cnt[:], bTf[:, NE:2 * NE], ALU.add).then_inc(sem("rank_used"), 1)
                                need(dve, sem("rank_used"), s.nR)
                    if s.G:
                        need(dve, sem("vn_full"), s.nG)
                        nc.vector.tensor_tensor(vn[:], bB[:], rows(beta[:]), ALU.mult).then_inc(sem("vn_ready"), 1)
                    if s.R:
                        for a in range(2):
                            ins = nc.vector.tensor_tensor_reduce(jr[:], oh[:, a, :], pre[:], 1.0, 0.0, ALU.mult, ALU.add,
                                                                 rt6[:, 2 + a:3 + a])
                            link(s, ins, 14 + a)
                        need(dve, sem("scattered"), 32 * s.pR)
                        nc.vector.scalar_tensor_tensor(out=posf[:], in0=rt6[:, 0:2], scalar=float(TCAP), in1=rt6[:, 2:4],
                                                       op0=ALU.mult, op1=ALU.add)
                        link(s, nc.vector.tensor_copy(toki[:], tokf[:]), 16)
                        link(s, nc.vector.tensor_scalar(tokf[:], tokf[:], float(P), None, ALU.add), 17)
                        nc.vector.tensor_copy(posi[:], posf[:]).then_inc(sem("pos_ready"), 1)
                        need(dve, sem("exp_ready"), 2 * s.nR)
                        link(s, nc.vector.scalar_tensor_tensor(out=rsm[:, 8:9], in0=rsm[:, 3:4], scalar=1.0, in1=rsm[:, 2:3],
                                                               op0=ALU.add, op1=ALU.mult), 18)
                        link(s, nc.vector.reciprocal(rt6[:, 4:5], rsm[:, 8:9]), 19)
                        link(s, nc.vector.tensor_tensor(rt6[:, 5:6], rt6[:, 4:5], rsm[:, 3:4], ALU.mult), 20)
                        nc.vector.tensor_copy(saved[:, bass.ds(s.pR, 1), :], rt6[:].unsqueeze(1)).then_inc(sem("saved_ready"), 1)
                    if s.G:
                        need(dve, sem("Su_full"), s.nG)
                        for h in range(H):
                            a = nc.vector.scalar_tensor_tensor(out=St[:, h, :], in0=St[:, h, :], scalar=eg8[:, 4 + h:5 + h],
                                                               in1=bA[:, h, :], op0=ALU.mult, op1=ALU.add)
                        a.then_inc(sem("S_new"), 1)
                        need(dve, sem("intra_full"), s.nG)
                        nc.vector.tensor_tensor(ot[:], ot[:], bC[:], ALU.add).then_inc(sem("o_ready"), 1)
                    if s.O:
                        need(dve, sem("wo_full"), s.nO)
                        need(dve, sem("x_res"), 16 * s.nO)
                        for half in range(2):
                            c = slice(512 * half, 512 * half + 512)
                            a = nc.vector.tensor_tensor(ht[:, c], ht[:, c], bOf[:, c], ALU.add)
                        a.then_inc(sem("h_ready"), 1)
                    if s.P:
                        need(dve, sem("gb_sq"), s.nP)
                        nc.vector.tensor_scalar(gg[:], gg[:], 0.044715, 1.0, ALU.mult, ALU.add).then_inc(sem("gelu_arg"), 1)
                        need(dve, sem("gelu_arg"), 2 * s.pP + 1)
                        nc.vector.tensor_tensor(gg[:], gg[:], pj[0][:], ALU.mult).then_inc(sem("gelu_arg"), 1)
                    if s.F:
                        need(dve, sem("x_turned"), s.nF)
                        need(dve, sem("ba_full"), s.nP)
                        for half in range(2):
                            k = 4 * half
                            a = nc.vector.tensor_tensor(uT[:, k:k + 4, :], bO[:, k:k + 4, :], rows(mg[:, k:k + 4]), ALU.mult)
                        a.then_inc(sem("uT_ready"), 1)
                    if s.O:
                        need(dve, sem("h_norm"), s.nO)
                        need(dve, sem("h_stored"), 16 * s.nO)
                        nc.vector.tensor_scalar(ht[:], ht[:], hst[:, 1:2], None, ALU.mult).then_inc(sem("u2_ready"), 1)
                    if s.G:
                        need(dve, sem("lrs_ready"), s.nG)
                        need(dve, sem("wo_full"), s.nO)
                        for j in range(4):
                            a = nc.vector.scalar_tensor_tensor(out=yl[:, j, :], in0=hh[:, j, :], scalar=lcol[:, 4, j:j + 1],
                                                               in1=lrs[:], op0=ALU.mult, op1=ALU.mult)
                        a.then_inc(sem("yl_ready"), 1)
                        need(dve, sem("o_norm"), s.nG)
                        need(dve, sem("zg_ready"), s.nG)
                        need(dve, sem("ydT_full"), s.nO)
                        for h in range(H):
                            a = nc.vector.scalar_tensor_tensor(out=yt[:, h, :], in0=ot[:, h, :], scalar=ors[:, h:h + 1],
                                                               in1=zg[:, h, :], op0=ALU.mult, op1=ALU.mult)
                        a.then_inc(sem("yt_ready"), 1)
                    if s.P:
                        need(dve, sem("gelu_sig"), s.nP)
                        nc.vector.tensor_tensor(gg[:], gg[:], pj[0][:], ALU.mult).then_inc(sem("gb_used"), 1)
                        need(dve, sem("z_sig"), s.nP)
                        nc.vector.tensor_tensor(zg[:], zg[:], pj[1][:], ALU.mult).then_inc(sem("z_used"), 1)
                        need(dve, sem("qkv_sig"), 3 * s.pP + 1)
                        nc.vector.tensor_tensor(ks[:], ks[:], ML[0][:], ALU.mult).then_inc(sem("k_silu"), 1)
                        need(dve, sem("qkv_sig"), 3 * s.pP + 2)
                        nc.vector.tensor_tensor(qs[:], qs[:], ML[1][:], ALU.mult).then_inc(sem("q_silu"), 1)
                        need(dve, sem("ba_full"), s.nP)
                        need(dve, sem("g_ready"), s.nG)
                        need(dve, sem("sgb_ready"), s.nP)
                        nc.vector.tensor_tensor(al[:], bTf[:, H:2 * H], dt_b[:], ALU.add).then_inc(sem("al_ready"), 1)
                        need(dve, sem("qkv_sig"), 3 * s.nP)
                        nc.vector.tensor_tensor(vs[:], vs[:], Mt[:], ALU.mult).then_inc(sem("v_silu"), 1)
                steps(dve, body)
                need(dve, sem("saved_ready"), TILES - 1)
                need(dve, sem("rank_used"), TILES - 1)

            @block.gpsimd
            def _(pool):
                def body(s):
                    if s.G:
                        need(pool, sem("g_ready"), s.nG)
                        need(pool, sem("Y_full"), 6 * s.pG)
                        nc.gpsimd.tensor_tensor(dec[:], cols(tri[:]), rows(g4[:]), ALU.mult).then_inc(sem("gtri_ready"), 1)
                        need(pool, sem("dec_exp"), s.nG)
                        nc.gpsimd.tensor_tensor(dec[:], dec[:], cols(tri[:]), ALU.mult).then_inc(sem("dec_ready"), 1)
                        need(pool, sem("M_raw"), s.nG)
                        need(pool, sem("beta_ready"), s.nG)
                        nc.gpsimd.tensor_tensor(Mt[:], Mt[:], rows(beta[:]), ALU.mult).then_inc(sem("M_ready"), 1)
                        need(pool, sem("M_ready"), s.nG)
                        need(pool, sem("vn_full"), s.pG)
                        nc.gpsimd.tensor_tensor(X[:], Mt[:], cols(lvl[:, 0, :]), ALU.mult).then_inc(sem("X_tmp"), 1)
                        need(pool, sem("ib_ready"), s.nG)
                        need(pool, sem("gx_ready"), s.nG)
                        b = nc.gpsimd.tensor_tensor(gx[:], gx[:], hh[:], ALU.mult)
                        if isinstance(s.i, int) and s.i == 0:
                            b.then_inc(sem("b_raw"), 1)
                            pool.wait_ge(sem("b_raw"), 1)
                            b = nc.gpsimd.memset(gx[:, :, 0:PAD], 0.0)
                        b.then_inc(sem("b_ready"), 1)
                    for l in LEVELS:
                        if s.G:
                            if l < 4:
                                need(pool, sem("k_silu"), s.pP)
                                need(pool, sem("q_silu"), s.pP)
                            else:
                                need(pool, sem("Y_full"), 6 * s.pG + l - 3)
                            nc.gpsimd.tensor_tensor(ML[l % 2][:], Mt[:], cols(lvl[:, l - 1, :]), ALU.mult).then_inc(sem("ML_ready"), 1)
                        if l == 4 and s.G:
                            need(pool, sem("hl_saved"), s.nG)
                            need(pool, sem("gb_used"), s.nG)
                            nc.gpsimd.tensor_tensor(hh[:], hh[:], gg[:], ALU.mult).then_inc(sem("y_lru"), 1)
                    if s.R:
                        if isinstance(s.i, int) and s.nR == 1:
                            pool.wait_ge(sem("idx_zeroed"), 16 * IDX_FILLS)
                        need(pool, sem("pos_ready"), s.nR)
                        settle(pool)
                        for a in range(2):
                            pool.indirect_dma_start(out=idx_tab, out_offset=bass.IndirectOffsetOnAxis(ap=posi[:, a:a + 1], axis=0),
                                                    in_=toki[:], in_offset=None).then_inc(sem("scattered"), 16)
                    if s.P:
                        need(pool, sem("r_gate"), s.nP)
                        nc.gpsimd.tensor_tensor(la, la, rows(cl[:]), ALU.mult).then_inc(sem("la_ready"), 1)
                        need(pool, sem("i_gate"), s.nP)
                        nc.gpsimd.tensor_tensor(gx[:], gx[:], xc[:], ALU.mult).then_inc(sem("gx_ready"), 1)
                        need(pool, sem("z_used"), s.nP)
                        nc.gpsimd.tensor_tensor(zg[:], zg[:], cols(dng[:]), ALU.mult).then_inc(sem("zg_ready"), 1)
                steps(pool, body)
                need(pool, sem("scattered"), 32 * (TILES - 1))

        retire(keep=["idx_zeroed", "scattered"] + [f"w_loaded{n}" for n in range(WSLOTS)])
        free = WSLOTS * SLOT + 2 * D
        room = W[:, free + 3 * FE:free + 3 * FE + 6 * NE].rearrange("p (n e) -> p n e", n=6)
        nb, end, start, ohb = (room[:, n, :] for n in range(4))
        ti, endi = (room[:, n, :].bitcast(I32) for n in (4, 5))
        tcol = sb("tcol", [P, 8])
        tcoli = sb("tcoli", [P, 4], I32)
        blk = W[0:1, free + 3 * FE + 6 * NE:free + 3 * FE + 6 * NE + 3 * P + 1].bitcast(I32)
        dstf = sb("dstf", [P, 2, SEQ // P])
        dsti = sb("dsti", [P, 2, SEQ // P], I32)
        NT = SEQ // P
        HT = NT // 2
        big = xc[:].rearrange("p a b -> p (a b)").rearrange("p (t e) -> p t e", e=NE)

        with nc.Block() as block:
            @block.vector
            def _(dve):
                done = [0]

                def link(ins):
                    done[0] += 1
                    ins.then_inc(sem("tab_step"), 1)
                    dve.wait_ge(sem("tab_step"), done[0])

                link(nc.vector.tensor_scalar(nb, cnt[:], 1.0 / P, (P - 1.0) / P - 0.5 + 0.5 / P, ALU.mult, ALU.add))
                link(nc.vector.tensor_copy(ti, nb))
                link(nc.vector.tensor_copy(nb, ti))
                link(nc.vector.memset(start, 0.0))
                link(nc.vector.tensor_tensor_scan(out=end[:], data0=nb[:], data1=start[:], initial=0.0, op0=ALU.add, op1=ALU.add))
                link(nc.vector.tensor_tensor(start, end, nb, ALU.subtract))
                nc.vector.tensor_scalar(endi, end, 1.0, None, ALU.add).then_inc(sem("end_ready"), 1)
                nc.vector.tensor_scalar(blk[:, 3 * P:3 * P + 1], end[0:1, NE - 1:NE], 0.5, -1.25, ALU.mult, ALU.add
                                        ).then_inc(sem("end_ready"), 1)
                link(nc.vector.tensor_scalar(ohb, end, iota_p[:], None, ALU.is_le))
                link(nc.vector.tensor_reduce(tcol[:, 0:1], ohb, AX, ALU.add))
                link(nc.vector.tensor_scalar(tcol[:, 0:1], tcol[:, 0:1], NE - 1.0, None, ALU.min))
                link(nc.vector.tensor_scalar(ohb, iota_e[:], tcol[:, 0:1], None, ALU.is_equal))
                link(nc.vector.tensor_tensor_reduce(nb, ohb, start, 1.0, 0.0, ALU.mult, ALU.add, tcol[:, 1:2]))
                link(nc.vector.tensor_tensor(tcol[:, 1:2], iota_p[:], tcol[:, 1:2], ALU.subtract))
                link(nc.vector.tensor_scalar(tcol[:, 1:2], tcol[:, 1:2], TCAP // P - 1.0, float(P), ALU.min, ALU.mult))
                link(nc.vector.scalar_tensor_tensor(out=tcol[:, 4:5], in0=tcol[:, 0:1], scalar=float(TCAP), in1=tcol[:, 1:2],
                                                    op0=ALU.mult, op1=ALU.add))
                link(nc.vector.tensor_scalar(tcol[:, 2:3], tcol[:, 0:1], 1.0, None, ALU.add))
                link(nc.vector.tensor_scalar(tcol[:, 5:6], tcol[:, 0:1], 1.0 / WSLOTS, 0.5 / WSLOTS - 0.5, ALU.mult, ALU.add))
                link(nc.vector.tensor_copy(tcoli[:, 0:1], tcol[:, 5:6]))
                link(nc.vector.tensor_copy(tcol[:, 5:6], tcoli[:, 0:1]))
                link(nc.vector.scalar_tensor_tensor(out=tcol[:, 3:4], in0=tcol[:, 5:6], scalar=-float(WSLOTS), in1=tcol[:, 0:1],
                                                    op0=ALU.mult, op1=ALU.add))
                link(nc.vector.tensor_scalar(tcol[:, 3:4], tcol[:, 3:4], float(SLOT), None, ALU.mult))
                nc.vector.tensor_copy(tcoli[:, 0:3], tcol[:, 2:5]).then_inc(sem("blk_ready"), 1)

            @block.sync
            def _(sp):
                sp.wait_ge(sem("blk_ready"), 1)
                sp.dma_start(blk_tab, tcoli[:, 0:3]).then_inc(sem("blk_out"), 16)
                sp.wait_ge(sem("blk_out"), 16)
                sp.dma_start(blk[:, 0:3 * P], blk_tab.rearrange("p c -> (p c)").unsqueeze(0)).then_inc(sem("blk_in"), 16)
                sp.wait_ge(sem("blk_in"), 16)
                sp.wait_ge(sem("end_ready"), 2)

        retire(keep=["idx_zeroed", "scattered"] + [f"w_loaded{n}" for n in range(WSLOTS)])
        xg = (x_in, ht)
        xT = uT
        hm = W[:, free:free + FE]
        sm = W[:, free + FE:free + 2 * FE]
        hm2 = W[:, free + 2 * FE:free + 3 * FE].rearrange("p (j n) -> p j n", j=2)
        yo = (W[:, WSLOTS * SLOT:WSLOTS * SLOT + D], W[:, WSLOTS * SLOT + D:WSLOTS * SLOT + 2 * D])
        gid = [sb(f"gid{n}", [P, 1], I32) for n in range(2)]

        def blocks(eng, body):
            for b in range(3):
                body(b, b % 2, False)
            stop = eng.value_load(blk[0:1, 3 * P:3 * P + 1], min_val=FEWEST, max_val=(NBLK - 2) // 2)
            with eng.Fori(1, (NBLK - 2) // 2) as p:
                with eng.If(p < stop):
                    body(1 + 2 * p, 1, False)
                    body(2 + 2 * p, 0, False)
            body(1 + 2 * stop, 1, False)
            body(2 + 2 * stop, 0, True)
            return stop

        def gathers(b, par):
            return 8 * b + (16 if par == 0 else 8)

        with nc.Block() as block:
            @block.sync
            def _(sp):
                for slot in range(WSLOTS - 1):
                    sp.wait_ge(sem(f"w_loaded{slot}"), 48)
                    sp.sem_inc(sem("w_ready"), 1)
                with sp.Fori(1, NE // WSLOTS) as q:
                    for slot in range(WSLOTS):
                        prev = (slot - 1) % WSLOTS
                        sp.wait_ge(sem(f"w_loaded{prev}"), 48 * q + (48 if slot else 0))
                        sp.sem_inc(sem("w_ready"), 1)
                        last = sp.value_load(endi[0:1, bass.ds((q - 1) * WSLOTS + slot, 1)], min_val=1, max_val=NBLK + 1)
                        sp.wait_ge(sem("y_full"), last)
                        settle(sp)
                        load_expert(sp, q * WSLOTS + slot, slot)
                sp.wait_ge(sem(f"w_loaded{WSLOTS - 1}"), 48 * (NE // WSLOTS))
                sp.sem_inc(sem("w_ready"), 1)

            @block.gpsimd
            def _(pool):
                def ids(b, par):
                    off = pool.value_load(blk[0:1, bass.ds(3 * b + 2, 1)], min_val=0, max_val=(NE - 1) * TCAP + TCAP - P)
                    pool.dma_start(gid[par][:], idx_tab[bass.ds(off, P), :]).then_inc(sem(f"gid_in{par}"), 16)

                def body(b, par, last):
                    if isinstance(b, int) and b == 0:
                        ids(0, 0)
                    pool.wait_ge(sem(f"gid_in{par}"), gathers(b, par))
                    need(pool, sem("xg_turned"), b - 1)
                    settle(pool)
                    pool.indirect_dma_start(out=xg[par][:], out_offset=None, in_=u_rows,
                                            in_offset=bass.IndirectOffsetOnAxis(ap=gid[par][:], axis=0)
                                            ).then_inc(sem(f"xg_in{par}"), 16)
                    if not last:
                        need(pool, sem(f"xg_in{1 - par}"), 8 * b + (0 if par == 0 else 8))
                        ids(b + 1, 1 - par)
                blocks(pool, body)

            @block.tensor
            def _(pe):
                def slot_of(b):
                    return pe.value_load(blk[0:1, bass.ds(3 * b + 1, 1)], min_val=0, max_val=(WSLOTS - 1) * SLOT)

                def turn_x(b, par):
                    pe.wait_ge(sem(f"xg_in{par}"), gathers(b, par))
                    need(pe, sem("xT_ready"), b)
                    for k in range(KT):
                        mm = pe.transpose(bO[:, k, :], xg[par][:, k:D:KT], ident[:])
                    mm.then_inc(sem("xg_turned"), 1)

                def down(b):
                    w = W[:, bass.ds(slot_of(b) + GU, WD)].rearrange("p (j n) -> p j n", j=2)
                    pe.wait_ge(sem("hm2_ready"), b + 1)
                    need(pe, sem("yo_a"), b)
                    need(pe, sem("yo_b"), b)
                    for half in range(2):
                        for j in range(2):
                            mm = pe.matmul(flat(pj[half]), hm2[:, j, :], w[:, j, 512 * half:512 * half + 512],
                                           start=(j == 0), stop=(j == 1))
                    mm.then_inc(sem("y_full"), 1)

                def body(b, par, last):
                    if isinstance(b, int) and b == 0:
                        turn_x(0, 0)
                    e1 = pe.value_load(blk[0:1, bass.ds(3 * b, 1)], min_val=1, max_val=NE)
                    w = W[:, bass.ds(slot_of(b), GU)].rearrange("p (g k f) -> p k g f", g=2, k=KT)
                    pe.wait_ge(sem("w_ready"), e1)
                    pe.wait_ge(sem("xT_ready"), b + 1)
                    need(pe, sem("hm_ready"), b)
                    for k in range(KT):
                        mm = pe.matmul(bA[:].rearrange("p a b -> p (a b)").rearrange("p (g f) -> p g f", g=2), xT[:, k, :],
                                       w[:, k], start=(k == 0), stop=(k == KT - 1))
                    mm.then_inc(sem("gu_full"), 1)
                    if not last:
                        turn_x(b + 1, 1 - par)
                    if not (isinstance(b, int) and b == 0):
                        down(b - 1)
                    pe.wait_ge(sem("hm_ready"), b + 1)
                    need(pe, sem("hm2_ready"), b)
                    for j in range(2):
                        mm = pe.transpose(bT[:, j, :], hm[:, j:FE:2], ident[:])
                    mm.then_inc(sem("hm_turned"), 1)
                    if last:
                        down(b)
                pe.sem_inc(sem("y_full"), 1)
                blocks(pe, body)

            @block.scalar
            def _(act):
                def out_half(b, par):
                    act.wait_ge(sem("y_full"), b + 2)
                    yo_free(b, par)
                    nc.scalar.activation(yo[par][:, 0:512], flat(pj[0]), ACT.Copy).then_inc(sem("yo_a"), 1)
                    act.wait_ge(sem("yo_a"), b + 1)
                    act.wait_ge(sem("yo_b"), b + 1)
                    act.dma_start(y_rows[bass.ds(b * P, P), :], yo[par]).then_inc(sem(f"y_stored{par}"), 16)

                def yo_free(b, par):
                    need(act, sem(f"y_stored{par}"), 8 * b - (8 if par else 0))

                def body(b, par, last):
                    act.wait_ge(sem("gu_full"), b + 1)
                    need(act, sem("hm_ready"), b)
                    nc.scalar.activation(sm, flat(bA)[:, 0:FE], ACT.Sigmoid).then_inc(sem("silu_sig"), 1)
                    if not (isinstance(b, int) and b == 0):
                        out_half(b - 1, 1 - par)
                    act.wait_ge(sem("hm_turned"), b + 1)
                    need(act, sem("y_full"), b + 1)
                    nc.scalar.activation(hm2, bT[:, 0:2, :], ACT.Copy).then_inc(sem("hm2_ready"), 1)
                    if last:
                        out_half(b, par)
                stop = blocks(act, body)
                act.wait_ge(sem("y_stored0"), 16 * stop + 32)
                settle(act)
                act.wait_ge(sem("y_stored1"), 16 * stop + 16)
                settle(act)

            @block.vector
            def _(dve):
                def turned(b):
                    dve.wait_ge(sem("xg_turned"), b + 1)
                    need(dve, sem("gu_full"), b)
                    for half in range(2):
                        k = 4 * half
                        a = nc.vector.tensor_tensor(xT[:, k:k + 4, :], bO[:, k:k + 4, :], rows(fg[:, k:k + 4]), ALU.mult)
                    a.then_inc(sem("xT_ready"), 1)

                def out_half(b, par):
                    dve.wait_ge(sem("y_full"), b + 2)
                    need(dve, sem(f"y_stored{par}"), 8 * b - (8 if par else 0))
                    nc.vector.tensor_copy(yo[par][:, 512:D], flat(pj[1])).then_inc(sem("yo_b"), 1)

                placed = [0]

                def place(a, half):
                    ts = slice(half * HT, half * HT + HT)
                    for ins in (
                        lambda: nc.vector.tensor_tensor(big, iota_e[:].unsqueeze(1).to_broadcast([P, HT, NE]),
                                                        saved[:, ts, a:a + 1].to_broadcast([P, HT, NE]), ALU.is_equal),
                        lambda: nc.vector.tensor_tensor(big, big, start.unsqueeze(1).to_broadcast([P, HT, NE]), ALU.mult),
                        lambda: nc.vector.tensor_reduce(dstf[:, a, ts], big, AX, ALU.add),
                        lambda: nc.vector.scalar_tensor_tensor(out=dstf[:, a, ts], in0=dstf[:, a, ts], scalar=float(P),
                                                               in1=saved[:, ts, 2 + a], op0=ALU.mult, op1=ALU.add),
                        lambda: nc.vector.tensor_copy(dsti[:, a, ts], dstf[:, a, ts]),
                    ):
                        ins().then_inc(sem("place_step"), 1)
                        placed[0] += 1
                        dve.wait_ge(sem("place_step"), placed[0])

                def body(b, par, last):
                    if isinstance(b, int) and b == 0:
                        turned(0)
                    dve.wait_ge(sem("silu_sig"), b + 1)
                    nc.vector.tensor_tensor(sm, sm, flat(bA)[:, 0:FE], ALU.mult).then_inc(sem("silu"), 1)
                    dve.wait_ge(sem("silu"), b + 1)
                    need(dve, sem("hm_turned"), b)
                    nc.vector.tensor_tensor(hm, sm, flat(bA)[:, FE:2 * FE], ALU.mult).then_inc(sem("hm_ready"), 1)
                    if not last:
                        turned(b + 1)
                    if not (isinstance(b, int) and b == 0):
                        out_half(b - 1, 1 - par)
                    if isinstance(b, int) and b < 2:
                        place(b, 0)
                        place(b, 1)
                    if last:
                        out_half(b, par)
                blocks(dve, body)

        NB = 4
        fgr = W[:, 0:D]
        ya, yb, hb, fo = ([W[:, (1 + NB * m + n) * D:(2 + NB * m + n) * D] for n in range(NB)] for m in range(4))
        di = [[sb(f"di{n}{a}", [P, 1], I32) for a in range(2)] for n in range(NB)]
        g2 = [sb(f"g2{n}", [P, 2]) for n in range(NB)]
        fst = sb("fst", [P, NB, 2])

        def tiles(eng, body, finish=None):
            def rounds(p):
                for par in range(NB):
                    body(p, NB * p + par, par)
                    if finish is not None and not (isinstance(p, int) and p == par == 0):
                        finish(*((p, NB * p + par - 1, par - 1) if par else (p - 1, NB * p - 1, NB - 1)))
            rounds(0)
            rounds(1)
            with eng.Fori(2, NT // NB) as p:
                rounds(p)
            if finish is not None:
                finish(NT // NB - 1, NT - 1, NB - 1)

        with nc.Block() as block:
            @block.sync
            def _(sp):
                sp.dma_start(fgr, final_g.partition_broadcast(P)).then_inc(sem("fg_in"), 16)

                def body(p, t, par):
                    need(sp, sem(f"h_used{par}"), p)
                    settle(sp)
                    sp.dma_start(hb[par], h_rows[bass.ds(t * P, P), :]).then_inc(sem(f"h_in{par}"), 16)
                tiles(sp, body)

            @block.gpsimd
            def _(pool):
                def body(p, t, par):
                    need(pool, sem(f"y0_in{par}"), 16 * p)
                    need(pool, sem(f"y1_in{par}"), 16 * p)
                    need(pool, sem(f"y_used{par}"), p)
                    settle(pool)
                    for a in range(2):
                        c = nc.gpsimd.tensor_copy(di[par][a][:], dsti[:, a, bass.ds(t, 1)])
                    c.then_inc(sem("di_ready"), 1)
                    pool.wait_ge(sem("di_ready"), t + 1)
                    settle(pool)
                    for a, y in enumerate((ya, yb)):
                        pool.indirect_dma_start(out=y[par], out_offset=None, in_=y_rows,
                                                in_offset=bass.IndirectOffsetOnAxis(ap=di[par][a][:], axis=0)
                                                ).then_inc(sem(f"y{a}_in{par}"), 16)
                tiles(pool, body)

            @block.scalar
            def _(act):
                def body(p, t, par):
                    act.wait_ge(sem("h2_ready"), t + 1)
                    need(act, sem(f"fo_ready{par}"), p)
                    nc.scalar.activation(junk[:], hb[par], ACT.Square, accum_out=fst[:, par, 0:1]).then_inc(sem("f_ss"), 1)
                    act.wait_ge(sem("f_ss"), t + 1)
                    nc.scalar.activation(fst[:, par, 1:2], fst[:, par, 0:1], ACT.Ln, scale=1.0 / D, bias=eps[:]).then_inc(sem("f_ln"), 1)
                    act.wait_ge(sem("f_ln"), t + 1)
                    nc.scalar.activation(fst[:, par, 1:2], fst[:, par, 1:2], ACT.Exp, scale=-0.5).then_inc(sem("f_norm"), 1)

                def store(p, t, par):
                    act.wait_ge(sem(f"fo_ready{par}"), p + 1)
                    act.dma_start(out[bass.ds(t * P, P), :], fo[par]).then_inc(sem(f"out{par}"), 16)
                tiles(act, body, store)
                for par in range(NB):
                    act.wait_ge(sem(f"out{par}"), 16 * (NT // NB))

            @block.vector
            def _(dve):
                dve.wait_ge(sem("fg_in"), 16)

                def body(p, t, par):
                    dve.wait_ge(sem(f"h_in{par}"), 16 * (p + 1))
                    dve.wait_ge(sem(f"y0_in{par}"), 16 * (p + 1))
                    nc.vector.tensor_copy(g2[par][:].unsqueeze(1), saved[:, bass.ds(t, 1), 4:6]).then_inc(sem("g2_ready"), 1)
                    dve.wait_ge(sem("g2_ready"), t + 1)
                    nc.vector.scalar_tensor_tensor(out=ya[par], in0=ya[par], scalar=g2[par][:, 0:1], in1=hb[par], op0=ALU.mult,
                                                   op1=ALU.add).then_inc(sem("h1_sum"), 1)
                    dve.wait_ge(sem("h1_sum"), t + 1)
                    dve.wait_ge(sem(f"y1_in{par}"), 16 * (p + 1))
                    nc.vector.scalar_tensor_tensor(out=hb[par], in0=yb[par], scalar=g2[par][:, 1:2], in1=ya[par], op0=ALU.mult,
                                                   op1=ALU.add).then_inc(sem("h2_ready"), 1)
                    dve.wait_ge(sem("h2_ready"), t + 1)
                    dve.sem_inc(sem(f"y_used{par}"), 1)

                def scaled(p, t, par):
                    dve.wait_ge(sem("f_norm"), t + 1)
                    need(dve, sem(f"out{par}"), 16 * p)
                    nc.vector.scalar_tensor_tensor(out=fo[par], in0=hb[par], scalar=fst[:, par, 1:2], in1=fgr, op0=ALU.mult,
                                                   op1=ALU.mult).then_inc(sem(f"fo_ready{par}"), 1)
                    dve.wait_ge(sem(f"fo_ready{par}"), p + 1)
                    dve.sem_inc(sem(f"h_used{par}"), 1)
                tiles(dve, body, scaled)


def kernel(**inputs):
    import numpy as np
    import concourse.bacc as bacc
    from concourse.bass_utils import run_bass_kernel_spmd

    a = {k: np.asarray(v) for k, v in inputs.items()}
    f32 = np.float32
    x = a["x"][0]

    def tiled(v):
        return v.reshape(-1, P).T

    arrays = {
        "xm": np.concatenate([np.zeros((PAD, D), x.dtype), a["meta_tokens"], x], axis=0),
        "w_in": a["w_in"][0],
        "w_out": a["w_out"][0],
        "conv_w": np.concatenate([a["lru_conv_w"][0], a["dn_conv_w"][0]], axis=1).reshape(CW, 16, P).transpose(2, 1, 0),
        "lru_cols": np.stack([tiled(a[n][0]) for n in ("lru_conv_b", "lru_b_r", "lru_b_i", "lru_lambda", "lru_out_norm")], axis=1),
        "w_r": a["lru_w_r"][0],
        "w_i": a["lru_w_i"][0],
        "mix_g": a["mix_norm"][0].reshape(P, KT),
        "ffn_g": a["ffn_norm"][0].reshape(P, KT),
        "final_g": a["final_norm"],
        "dn_g": a["dn_out_norm"][0],
        "dn_a": a["dn_a_log"][0],
        "dn_dt": a["dn_dt_bias"][0],
        "w_router": np.concatenate([a["router_group_w"][0], a["router_expert_w"][0]], axis=1),
        "b_router": np.concatenate([a["router_group_b"][0], a["router_expert_b"][0]], axis=0),
        "w_gate": a["moe_w_gate"][0],
        "w_up": a["moe_w_up"][0],
        "w_down": a["moe_w_down"][0],
    }
    arrays = {k: np.ascontiguousarray(v) for k, v in arrays.items()}
    nc = bacc.Bacc("TRN2", target_bir_lowering=False, num_devices=1, dynamic_dma_scratch_size=4096)
    args = [nc.dram_tensor(k, v.shape, mybir.dt.from_np(v.dtype), kind="ExternalInput").ap() for k, v in arrays.items()]
    out = nc.dram_tensor("out", (SEQ, D), F32, kind="ExternalOutput").ap()
    hymba_block(nc, *args, out)
    r = run_bass_kernel_spmd(nc, [arrays], core_ids=[0])
    return r.results[0]["out"].reshape(1, SEQ, D)
```
